# Optimizing a Trainium2 kernel written in Bass

```python
import math
import jax, jax.numpy as jnp
from jax import lax
import numpy as np

D_MODEL = 2048
BATCH = 1
SEQ = 256
DEPTH = 2
DEC_BATCH = 8
DEC_SEQ = 4
PAST_LEN = 2048
PAGE_SIZE = 128

EXPAND = 2
D_INNER = EXPAND * D_MODEL
N_AB = (DEPTH + 1) // 2
N_C = DEPTH // 2
CHUNK = 64
EPS = 1e-6
GLA_WIDTH = D_INNER // 2
GLA_HEADS = 4
GLA_DK = GLA_WIDTH // 2 // GLA_HEADS
GLA_DV = GLA_WIDTH // GLA_HEADS
GLA_QK = GLA_HEADS * GLA_DK
GLA_LOWRANK = 16
GLA_GATE_TEMP = 16.0
ML_WIDTH = D_INNER // 2
ML_HEADS = 4
ML_DK = ML_WIDTH // 2 // ML_HEADS
ML_DV = ML_WIDTH // ML_HEADS
ML_QK = ML_HEADS * ML_DK
ML_CONV = 4
AB_SPLITS = (GLA_QK, GLA_QK, GLA_WIDTH, GLA_WIDTH, GLA_LOWRANK,
             ML_QK, ML_QK, ML_WIDTH, ML_WIDTH, ML_WIDTH, ML_HEADS, ML_HEADS)
AB_IN = 2 * GLA_QK + 2 * GLA_WIDTH + GLA_LOWRANK + 2 * ML_QK + 3 * ML_WIDTH + 2 * ML_HEADS
SSD_HEAD_DIM = 64
SSD_HEADS = D_INNER // SSD_HEAD_DIM
SSD_GROUPS = 8
SSD_HPG = SSD_HEADS // SSD_GROUPS
SSD_STATE = 128
SSD_CONV = 4
SSD_CONV_DIM = D_INNER + 2 * SSD_GROUPS * SSD_STATE
C_IN = D_INNER + SSD_CONV_DIM + SSD_HEADS

kernel_name = 'hybrid_gla_mlstm_ssd_decode_step'

F32 = jnp.float32

def _rms(x):
    return x * lax.rsqrt(jnp.mean(jnp.square(x), axis=-1, keepdims=True) + EPS)

def rmsnorm(x, w):
    return (_rms(x.astype(F32)) * w.astype(F32)).astype(x.dtype)

def _split(t, sizes):
    out, o = [], 0
    for s in sizes:
        out.append(t[..., o:o + s])
        o += s
    return out

def to_chunks(t, c):
    b, l = t.shape[:2]
    return jnp.swapaxes(t.reshape((b, l // c, c) + t.shape[2:]), 0, 1)

def from_chunks(t):
    n, b, c = t.shape[:3]
    return jnp.swapaxes(t, 0, 1).reshape((b, n * c) + t.shape[3:])

def causal_conv(x, buf, w, b):
    k_w = w.shape[0]
    L = x.shape[1]
    xp = jnp.concatenate([buf.astype(x.dtype), x], axis=1)
    out = xp[:, 0:L] * w[0]
    for t in range(1, k_w):
        out = out + xp[:, t:t + L] * w[t]
    return out + b, xp[:, L:]

def gla_scan(q, k, v, g, s0):
    L = q.shape[1]
    c = math.gcd(L, CHUNK)
    q = q * (q.shape[-1] ** -0.5)
    mask = jnp.tril(jnp.ones((c, c), dtype=bool))

    def step(s, inp):
        qc, kc, vc, gc = inp
        b = jnp.cumsum(gc, axis=1)
        mid = b[:, c // 2][:, None]
        b_last = b[:, -1]
        o_inter = jnp.einsum('bihk,bhkv->bihv', qc * jnp.exp(b), s)
        att = jnp.einsum('bihk,bjhk->bhij', qc * jnp.exp(b - mid), kc * jnp.exp(mid - b))
        att = jnp.where(mask, att, 0.0)
        o_intra = jnp.einsum('bhij,bjhv->bihv', att, vc)
        s_new = jnp.exp(b_last)[..., None] * s + jnp.einsum(
            'bjhk,bjhv->bhkv', kc * jnp.exp(b_last[:, None] - b), vc)
        return s_new, o_inter + o_intra

    s_fin, o = lax.scan(step, s0, tuple(to_chunks(t, c) for t in (q, k, v, g)))
    return from_chunks(o), s_fin

def mlstm_scan(q, k, v, ig, fg, c0, n0, m0):
    L = q.shape[1]
    c = math.gcd(L, CHUNK)
    k = k * (k.shape[-1] ** -0.5)
    logf = jax.nn.log_sigmoid(fg)
    mask = jnp.tril(jnp.ones((c, c), dtype=bool))

    def step(carry, inp):
        cm, nm, mm = carry
        qc, kc, vc, ic, lfc = inp
        fcum = jnp.swapaxes(jnp.cumsum(lfc, axis=1), 1, 2)
        it = jnp.swapaxes(ic, 1, 2)
        dlog = jnp.where(mask, fcum[..., :, None] - fcum[..., None, :] + it[..., None, :], -jnp.inf)
        inter = fcum + mm[..., None]
        m_i = jnp.maximum(inter, jnp.max(dlog, axis=-1))
        w_inter = jnp.exp(inter - m_i)
        qk = jnp.einsum('bihk,bjhk->bhij', qc, kc) * jnp.exp(dlog - m_i[..., None])
        num = jnp.einsum('bhij,bjhv->bihv', qk, vc) + jnp.swapaxes(w_inter, 1, 2)[..., None] * \
            jnp.einsum('bihk,bhkv->bihv', qc, cm)
        den = jnp.sum(qk, axis=-1) + w_inter * jnp.einsum('bihk,bhk->bhi', qc, nm)
        den = jnp.maximum(jnp.abs(den), jnp.exp(-m_i))
        h = num / jnp.swapaxes(den, 1, 2)[..., None]
        m_new = m_i[..., -1]
        w_j = jnp.exp(fcum[..., -1:] - fcum + it - m_new[..., None])
        decay = jnp.exp(fcum[..., -1] + mm - m_new)
        c_new = decay[..., None, None] * cm + jnp.einsum('bhj,bjhk,bjhv->bhkv', w_j, kc, vc)
        n_new = decay[..., None] * nm + jnp.einsum('bhj,bjhk->bhk', w_j, kc)
        return (c_new, n_new, m_new), h

    (c_f, n_f, m_f), h = lax.scan(step, (c0, n0, m0),
                                  tuple(to_chunks(t, c) for t in (q, k, v, ig, logf)))
    return from_chunks(h), c_f, n_f, m_f

def ssd_scan(x, dt, a, bm, cm, s0):
    L = x.shape[1]
    c = math.gcd(L, CHUNK)
    mask = jnp.tril(jnp.ones((c, c), dtype=bool))[None, :, :, None, None]

    def step(s, inp):
        xc, dtc, bc, cc = inp
        acum = jnp.cumsum(dtc * a, axis=1)
        seg = acum[:, :, None] - acum[:, None, :]
        decay = jnp.exp(jnp.where(mask, seg, -jnp.inf))
        cb = jnp.einsum('bign,bjgn->bijg', cc, bc)
        y_intra = jnp.einsum('bijgh,bjghp->bighp', cb[..., None] * decay, dtc[..., None] * xc)
        y_inter = jnp.einsum('bign,bghpn->bighp', cc, s) * jnp.exp(acum)[..., None]
        a_last = acum[:, -1]
        w = jnp.exp(a_last[:, None] - acum) * dtc
        s_new = jnp.exp(a_last)[..., None, None] * s + jnp.einsum('bjgh,bjghp,bjgn->bghpn', w, xc, bc)
        return s_new, y_intra + y_inter

    s_fin, y = lax.scan(step, s0, tuple(to_chunks(t, c) for t in (x, dt, bm, cm)))
    return from_chunks(y), s_fin

def ab_mixer(h, s_gla, s_mc, s_mn, s_mm, s_mconv, w_in, gla_w_a2, gla_b_a, gla_norm,
             ml_conv_w, ml_conv_b, ml_b_i, ml_b_f, ml_norm, w_out):
    bsz, L, _ = h.shape
    proj = h @ w_in
    qg, kg, vg, zg, ag, qm, km, vm, om, zm, im, fm = _split(proj, AB_SPLITS)
    gate = jax.nn.log_sigmoid((ag @ gla_w_a2 + gla_b_a).astype(F32)) / GLA_GATE_TEMP
    hd = lambda t, d: t.astype(F32).reshape(bsz, L, -1, d)
    o_g, s_gla_new = gla_scan(hd(qg, GLA_DK), hd(kg, GLA_DK), hd(vg, GLA_DV), hd(gate, GLA_DK),
                              s_gla.astype(F32))
    o_g = (_rms(o_g) * gla_norm.astype(F32).reshape(GLA_HEADS, GLA_DV)).reshape(bsz, L, GLA_WIDTH)
    o_g = o_g * jax.nn.silu(zg.astype(F32))
    qk_c, mconv_new = causal_conv(jnp.concatenate([qm, km], axis=-1), s_mconv, ml_conv_w, ml_conv_b)
    qk_c = jax.nn.silu(qk_c.astype(F32))
    q_m, k_m = _split(qk_c, (ML_QK, ML_QK))
    h_m, c_new, n_new, m_new = mlstm_scan(
        hd(q_m, ML_DK), hd(k_m, ML_DK), hd(vm, ML_DV),
        (im + ml_b_i).astype(F32), (fm + ml_b_f).astype(F32),
        s_mc.astype(F32), s_mn.astype(F32), s_mm.astype(F32))
    h_m = jax.nn.sigmoid(hd(om, ML_DV)) * h_m
    h_m = (_rms(h_m) * ml_norm.astype(F32).reshape(ML_HEADS, ML_DV)).reshape(bsz, L, ML_WIDTH)
    h_m = h_m * jax.nn.silu(zm.astype(F32))
    y = jnp.concatenate([o_g, h_m], axis=-1).astype(h.dtype) @ w_out
    return y, s_gla_new, c_new, n_new, m_new, mconv_new

def c_mixer(h, s_ssm, s_conv, w_in, conv_w, conv_b, dt_bias, a_log, d_skip, norm_w, w_out):
    bsz, L, _ = h.shape
    proj = h @ w_in
    z, xbc, dt = _split(proj, (D_INNER, SSD_CONV_DIM, SSD_HEADS))
    xbc, conv_new = causal_conv(xbc, s_conv, conv_w, conv_b)
    xbc = jax.nn.silu(xbc.astype(F32))
    xs, bm, cm = _split(xbc, (D_INNER, SSD_GROUPS * SSD_STATE, SSD_GROUPS * SSD_STATE))
    xs = xs.reshape(bsz, L, SSD_GROUPS, SSD_HPG, SSD_HEAD_DIM)
    bm = bm.reshape(bsz, L, SSD_GROUPS, SSD_STATE)
    cm = cm.reshape(bsz, L, SSD_GROUPS, SSD_STATE)
    dt = jax.nn.softplus(dt.astype(F32) + dt_bias.astype(F32)).reshape(bsz, L, SSD_GROUPS, SSD_HPG)
    a = -jnp.exp(a_log.astype(F32)).reshape(SSD_GROUPS, SSD_HPG)
    s0 = s_ssm.astype(F32).reshape(bsz, SSD_GROUPS, SSD_HPG, SSD_HEAD_DIM, SSD_STATE)
    y, s_new = ssd_scan(xs, dt, a, bm, cm, s0)
    y = y + d_skip.astype(F32).reshape(SSD_GROUPS, SSD_HPG)[..., None] * xs
    y = y.reshape(bsz, L, D_INNER) * jax.nn.silu(z.astype(F32))
    y = _rms(y.reshape(bsz, L, SSD_GROUPS, D_INNER // SSD_GROUPS)).reshape(bsz, L, D_INNER)
    y = (y * norm_w.astype(F32)).astype(h.dtype) @ w_out
    return y, s_new.reshape(bsz, SSD_HEADS, SSD_HEAD_DIM, SSD_STATE), conv_new

def trunk(x, s_gla, s_mc, s_mn, s_mm, s_mconv, s_ssm, s_sconv, p):
    gla_l, mc_l, mn_l, mm_l, mcv_l, ssm_l, scv_l = [], [], [], [], [], [], []
    for layer in range(DEPTH):
        i = layer // 2
        if layer % 2 == 0:
            y, sg, sc, sn, sm, scv = ab_mixer(
                rmsnorm(x, p['norm_ab'][i]), s_gla[i], s_mc[i], s_mn[i], s_mm[i], s_mconv[i],
                p['w_in_ab'][i], p['gla_w_a2'][i], p['gla_b_a'][i], p['gla_norm'][i],
                p['mlstm_conv_w'][i], p['mlstm_conv_b'][i], p['mlstm_b_i'][i], p['mlstm_b_f'][i],
                p['mlstm_norm'][i], p['w_out_ab'][i])
            gla_l.append(sg); mc_l.append(sc); mn_l.append(sn); mm_l.append(sm); mcv_l.append(scv)
        else:
            y, ss, sv = c_mixer(
                rmsnorm(x, p['norm_c'][i]), s_ssm[i], s_sconv[i], p['w_in_c'][i],
                p['ssd_conv_w'][i], p['ssd_conv_b'][i], p['ssd_dt_bias'][i], p['ssd_a_log'][i],
                p['ssd_d'][i], p['ssd_norm'][i], p['w_out_c'][i])
            ssm_l.append(ss); scv_l.append(sv)
        x = x + y
    return (rmsnorm(x, p['final_norm']), jnp.stack(gla_l), jnp.stack(mc_l), jnp.stack(mn_l),
            jnp.stack(mm_l), jnp.stack(mcv_l), jnp.stack(ssm_l), jnp.stack(scv_l))

def setup_inputs(seed: int = 0) -> dict:
    key = jax.random.key(seed)
    ks = jax.random.split(key, 32)
    nrm = lambda k, shape, scale: jax.random.normal(k, shape, F32) * scale
    dt0 = jnp.exp(jax.random.uniform(ks[25], (N_C, SSD_HEADS), F32) * (math.log(0.1) - math.log(0.001))
                  + math.log(0.001))
    return {
        'x_prompt': nrm(ks[0], (BATCH, SEQ, D_MODEL), 1.0),
        'x_sample': nrm(ks[1], (DEC_BATCH, DEC_SEQ, D_MODEL), 1.0),
        'state_gla': nrm(ks[2], (N_AB, DEC_BATCH, GLA_HEADS, GLA_DK, GLA_DV), 0.1),
        'state_mlstm_c': nrm(ks[3], (N_AB, DEC_BATCH, ML_HEADS, ML_DK, ML_DV), 0.1),
        'state_mlstm_n': nrm(ks[4], (N_AB, DEC_BATCH, ML_HEADS, ML_DK), 0.5),
        'state_mlstm_m': jax.random.uniform(ks[5], (N_AB, DEC_BATCH, ML_HEADS), F32, 0.0, 4.0),
        'state_mlstm_conv': nrm(ks[6], (N_AB, DEC_BATCH, ML_CONV - 1, 2 * ML_QK), 1.0),
        'state_ssm': nrm(ks[7], (N_C, DEC_BATCH, SSD_HEADS, SSD_HEAD_DIM, SSD_STATE), 0.1),
        'state_ssm_conv': nrm(ks[8], (N_C, DEC_BATCH, SSD_CONV - 1, SSD_CONV_DIM), 1.0),
        'norm_ab': 1.0 + nrm(ks[9], (N_AB, D_MODEL), 0.02),
        'w_in_ab': nrm(ks[10], (N_AB, D_MODEL, AB_IN), D_MODEL ** -0.5),
        'gla_w_a2': nrm(ks[11], (N_AB, GLA_LOWRANK, GLA_QK), GLA_LOWRANK ** -0.5),
        'gla_b_a': nrm(ks[12], (N_AB, GLA_QK), 0.1),
        'gla_norm': 1.0 + nrm(ks[13], (N_AB, GLA_WIDTH), 0.02),
        'mlstm_conv_w': nrm(ks[14], (N_AB, ML_CONV, 2 * ML_QK), ML_CONV ** -0.5),
        'mlstm_conv_b': nrm(ks[15], (N_AB, 2 * ML_QK), 0.02),
        'mlstm_b_i': nrm(ks[16], (N_AB, ML_HEADS), 0.1),
        'mlstm_b_f': jnp.linspace(3.0, 6.0, ML_HEADS, dtype=F32) + nrm(ks[17], (N_AB, ML_HEADS), 0.1),
        'mlstm_norm': 1.0 + nrm(ks[18], (N_AB, ML_WIDTH), 0.02),
        'w_out_ab': nrm(ks[19], (N_AB, D_INNER, D_MODEL), D_INNER ** -0.5),
        'norm_c': 1.0 + nrm(ks[20], (N_C, D_MODEL), 0.02),
        'w_in_c': nrm(ks[21], (N_C, D_MODEL, C_IN), D_MODEL ** -0.5),
        'ssd_conv_w': nrm(ks[22], (N_C, SSD_CONV, SSD_CONV_DIM), SSD_CONV ** -0.5),
        'ssd_conv_b': nrm(ks[23], (N_C, SSD_CONV_DIM), 0.02),
        'ssd_dt_bias': dt0 + jnp.log(-jnp.expm1(-dt0)),
        'ssd_a_log': jnp.log(jax.random.uniform(ks[24], (N_C, SSD_HEADS), F32, 1.0, 16.0)),
        'ssd_d': 1.0 + nrm(ks[26], (N_C, SSD_HEADS), 0.1),
        'ssd_norm': 1.0 + nrm(ks[27], (N_C, D_INNER), 0.02),
        'w_out_c': nrm(ks[28], (N_C, D_INNER, D_MODEL), D_INNER ** -0.5),
        'final_norm': 1.0 + nrm(ks[29], (D_MODEL,), 0.02),
    }

def reference(x_prompt, x_sample, state_gla, state_mlstm_c, state_mlstm_n, state_mlstm_m,
              state_mlstm_conv, state_ssm, state_ssm_conv, norm_ab, w_in_ab, gla_w_a2, gla_b_a,
              gla_norm, mlstm_conv_w, mlstm_conv_b, mlstm_b_i, mlstm_b_f, mlstm_norm, w_out_ab,
              norm_c, w_in_c, ssd_conv_w, ssd_conv_b, ssd_dt_bias, ssd_a_log, ssd_d, ssd_norm,
              w_out_c, final_norm):
    p = dict(norm_ab=norm_ab, w_in_ab=w_in_ab, gla_w_a2=gla_w_a2, gla_b_a=gla_b_a, gla_norm=gla_norm,
             mlstm_conv_w=mlstm_conv_w, mlstm_conv_b=mlstm_conv_b, mlstm_b_i=mlstm_b_i,
             mlstm_b_f=mlstm_b_f, mlstm_norm=mlstm_norm, w_out_ab=w_out_ab, norm_c=norm_c,
             w_in_c=w_in_c, ssd_conv_w=ssd_conv_w, ssd_conv_b=ssd_conv_b, ssd_dt_bias=ssd_dt_bias,
             ssd_a_log=ssd_a_log, ssd_d=ssd_d, ssd_norm=ssd_norm, w_out_c=w_out_c,
             final_norm=final_norm)
    bp = x_prompt.shape[0]
    y_prompt, gla_p, mc_p, mn_p, mm_p, mcv_p, ssm_p, scv_p = trunk(
        x_prompt,
        jnp.zeros((N_AB, bp, GLA_HEADS, GLA_DK, GLA_DV), F32),
        jnp.zeros((N_AB, bp, ML_HEADS, ML_DK, ML_DV), F32),
        jnp.zeros((N_AB, bp, ML_HEADS, ML_DK), F32),
        jnp.zeros((N_AB, bp, ML_HEADS), F32),
        jnp.zeros((N_AB, bp, ML_CONV - 1, 2 * ML_QK), x_prompt.dtype),
        jnp.zeros((N_C, bp, SSD_HEADS, SSD_HEAD_DIM, SSD_STATE), F32),
        jnp.zeros((N_C, bp, SSD_CONV - 1, SSD_CONV_DIM), x_prompt.dtype),
        p)
    y_sample, gla_s, mc_s, mn_s, mm_s, mcv_s, ssm_s, scv_s = trunk(
        x_sample, state_gla, state_mlstm_c, state_mlstm_n, state_mlstm_m, state_mlstm_conv,
        state_ssm, state_ssm_conv, p)
    return (y_prompt, y_sample, gla_p, gla_s, mc_p, mc_s, mn_p, mn_s, mm_p, mm_s,
            mcv_p, mcv_s, ssm_p, ssm_s, scv_p, scv_s)


_drawn_inputs = setup_inputs


def setup_inputs(seed=0):
    import zlib

    import numpy as np

    out = dict(_drawn_inputs(seed))
    spreads = {}
    factors = {'gla_norm': 4.068, 'mlstm_norm': 4.331, 'ssd_norm': 4.245, 'final_norm': 2.849}
    for name, (base, spread) in spreads.items():
        noise = np.random.default_rng([zlib.crc32(name.encode()), seed]).standard_normal(out[name].shape)
        drawn = base * np.exp(spread * noise) if base else spread * noise
        out[name] = __import__('jax').numpy.asarray(drawn.astype(out[name].dtype))
    for name, factor in factors.items():
        out[name] = (out[name] * factor).astype(out[name].dtype)
    return out
```

```python
from contextlib import ExitStack

import concourse.bass as bass
import numpy as np
from concourse import mybir
from concourse.alu_op_type import AluOpType as ALU

F32 = mybir.dt.float32
F32R = mybir.dt.float32r
U32 = mybir.dt.uint32
ACT = mybir.ActivationFunctionType

P = 128
D = 2048
TP, NB, TD = 256, 8, 4
TS = NB * TD
T = TP + TS
S0 = TP
KT = D // P
HD = 4
DK, DV = 256, 512
GW = 256
UK = 4
UNITS = 4
RAW = 4
EPS = 1e-6
CH = 64
SSD_H, SSD_P, SSD_N, SSD_G = 64, 64, 128, 8
CT = 48

C_NAB, C_NC, C_FN, C_GN, C_MN, C_BA, C_MCB = 0, 16, 32, 48, 64, 80, 88
C_MCW, C_SN, C_D = 128, 192, 224
C_SCW, C_SCB = 256, 512


def scw_col(tap):
    return C_SCW + (tap // 2) * 128 + (tap % 2) * CT


class Steps:

    def __init__(self, eng, sem):
        self.eng, self.sem, self.n = eng, sem, 0

    def then_wait(self, ins):
        ins.then_inc(self.sem, 1)
        self.n += 1
        self.eng.wait_ge(self.sem, self.n)

    def restart(self):
        self.eng.sem_clear(self.sem)
        self.n = 0


class Core:

    def __init__(self, nc, ctx):
        self.nc, self.ctx = nc, ctx
        sb, ps = self.sb, self.ps
        self.xn_hi = sb("xn_hi", [P, KT, T], F32R)
        self.xn_lo = sb("xn_lo", [P, KT, T], F32R)
        self.w_raw = sb("w_raw", [P, RAW, UK, GW])
        self.w_hi = sb("w_hi", [P, UNITS, UK, GW], F32R)
        self.w_lo = sb("w_lo", [P, UNITS, UK, GW], F32R)
        self.ident = sb("ident", [P, P])
        self.ones = sb("ones", [P, P])
        self.tri = sb("tri", [P, P])
        self.smask = sb("smask", [P, TS])
        self.seg = sb("seg", [P, NB])
        self.keep = sb("keep", [P, T])
        self.parT = sb("parT", [P, 640])
        self.bank = [ps(f"bank{i}", [P, 512]) for i in range(8)]

    def sb(self, name, shape, dt=F32, ctx=None):
        return (ctx or self.ctx).enter_context(self.nc.sbuf_tensor(name, shape, dt))

    def ps(self, name, shape):
        return self.ctx.enter_context(self.nc.psum_tensor(name, shape, F32))


def weight_sems(sem, tag):
    return dict(arrived=[sem(f"{tag}_w_arrived{j}") for j in range(RAW)], hi=sem(f"{tag}_w_hi"),
                split=sem(f"{tag}_w_split"), used=sem(f"{tag}_w_used"), turns=sem(f"{tag}_w_turns"))




def load_unit(sp, core, ws, quad, j, src):
    sp.wait_ge(ws["split"], quad * UNITS + (j + 1))
    sp.sem_inc(ws["turns"], 1)
    sp.dma_start(core.w_raw[:, j % RAW], src).then_inc(ws["arrived"][j % RAW], 16)


def split_hi_unit(act, core, ws, quad, j):
    act.wait_ge(ws["arrived"][j % RAW], quad * (16 * UNITS // RAW) + 16 * (j // RAW + 1))
    act.wait_ge(ws["used"], quad * UNITS + (j + 1))
    act.activation(core.w_hi[:, j], core.w_raw[:, j % RAW], ACT.Copy).then_inc(ws["hi"], 1)


def split_lo_unit(dve, core, ws, quad, j):
    dve.wait_ge(ws["hi"], quad * UNITS + (j + 1))
    dve.tensor_tensor(core.w_lo[:, j], core.w_raw[:, j % RAW], core.w_hi[:, j].bitcast(F32),
                      ALU.subtract).then_inc(ws["split"], 1)


def project_unit(pe, core, ws, quad, j, hi, lo, kt0, banks, first, last):
    pe.wait_ge(ws["split"], quad * UNITS + (j + 1 + RAW))
    for m in range(2):
        for kk in range(UK):
            k = kt0 + UK * j + kk
            col = slice(P * m, P * m + P)
            f = first and j == 0 and kk == 0
            e = last and j == UNITS - 1 and kk == UK - 1
            pe.matmul(banks[m][:, 0:T], core.w_hi[:, j, kk, col], hi[:, k], start=f, stop=False)
            pe.matmul(banks[m][:, 0:T], core.w_hi[:, j, kk, col], lo[:, k], start=False, stop=False)
            ins = pe.matmul(banks[m][:, 0:T], core.w_lo[:, j, kk, col], hi[:, k], start=False, stop=e)
    ins.then_inc(ws["used"], 1)


def split_hi(act, core, ws, quad):
    for j in range(UNITS):
        split_hi_unit(act, core, ws, quad, j)


def split_lo(dve, core, ws, quad):
    for j in range(UNITS):
        split_lo_unit(dve, core, ws, quad, j)


def rsqrt_act(act, out, var, steps):
    steps.then_wait(act.activation(out, var, ACT.Ln))
    return act.activation(out, out, ACT.Exp, scale=-0.5)


def rsqrt_newton(dve, r, var, tmp, steps):
    steps.then_wait(dve.tensor_tensor(tmp, r, r, ALU.mult))
    steps.then_wait(dve.scalar_tensor_tensor(tmp, tmp, -0.5, var, ALU.mult, ALU.mult))
    return dve.scalar_tensor_tensor(r, tmp, 1.5, r, ALU.add, ALU.mult)


def samples(ap, width=TD):
    return ap.rearrange("p (b t) -> p b t", t=width)


def samples2(ap, width=TD):
    return ap.rearrange("p k (b t) -> p k b t", t=width)


class NormJob:

    def __init__(self, core, sem, tag, xT, wcol, sq, var, r, tmp, y=None):
        self.core, self.xT, self.wcol, self.y = core, xT, wcol, y
        self.sq, self.var, self.r, self.tmp = sq, var, r, tmp
        self.ready, self.squared, self.scaled, self.high, self.var_ok, self.r0, self.done, self.sq_free = (
            sem(f"{tag}_{n}") for n in "x_ready squared scaled high variance r_first normed sq_free".split())
        self.stored = [sem(f"{tag}_x_stored{q}") for q in range(KT // 4)]

    def store(self, sp, dst, q):
        sp.wait_ge(self.ready, 4 * q + 4)
        sp.dma_start(dst[:, 4 * q:4 * q + 4], self.xT[:, 4 * q:4 * q + 4]).then_inc(self.stored[q], 16)

    def scalar_square(self, act, k, wait):
        if k >= 4:
            act.wait_ge(self.sq_free, k - 3)
        act.wait_ge(self.ready, wait)
        act.activation(self.sq[:, k % 4], self.xT[:, k], ACT.Square).then_inc(self.squared, 1)

    def tensor_sum(self, pe, bank, k):
        pe.wait_ge(self.squared, k + 1)
        pe.matmul(bank[:, 0:T], self.core.ones[:], self.sq[:, k % 4], start=k == 0, stop=k == KT - 1,
                  skip_group_check=True).then_inc(self.sq_free, 1)

    def scalar_r(self, act, steps):
        act.wait_ge(self.var_ok, 1)
        rsqrt_act(act, self.r[:], self.var[:], steps).then_inc(self.r0, 1)
        if self.y is None:
            for i in range(0, KT, 4):
                act.wait_ge(self.scaled, i // 4 + 1)
                act.activation(self.core.xn_hi[:, i:i + 4], self.xT[:, i:i + 4], ACT.Copy).then_inc(self.high, 1)

    def vector(self, dve, bank, steps):
        dve.wait_ge(self.sq_free, KT)
        dve.tensor_scalar(self.var[:], bank[:, 0:T], 1.0 / D, EPS, ALU.mult, ALU.add).then_inc(self.var_ok, 1)
        dve.wait_ge(self.r0, 1)
        steps.then_wait(rsqrt_newton(dve, self.r[:], self.var[:], self.tmp[:], steps))
        c = self.core
        for k in range(KT):
            if self.y is None and k % 4 == 0:
                dve.wait_ge(self.stored[k // 4], 16)
            w = c.parT[:, self.wcol + k:self.wcol + k + 1]
            x = self.xT[:, k]
            ins = dve.scalar_tensor_tensor(x, x, w, self.r[:], ALU.mult, ALU.mult)
            if self.y is not None:
                ins.then_inc(self.done, 1)
            elif k % 4 == 3:
                ins.then_inc(self.scaled, 1)
            if self.y is None and k % 4 == 3 and k > 3:
                self.rest(dve, k - 7)
        if self.y is None:
            self.rest(dve, KT - 4)

    def rest(self, dve, k):
        c = self.core
        dve.wait_ge(self.high, k // 4 + 1)
        dve.tensor_tensor(c.xn_lo[:, k:k + 4], self.xT[:, k:k + 4], c.xn_hi[:, k:k + 4].bitcast(F32), ALU.subtract
                          ).then_inc(self.done, 1)


def gate_product(pe, core, hi, lo, out, normed, done):
    for k in range(KT):
        if k % 4 == 0:
            pe.wait_ge(normed, k // 4 + 1)
        pe.matmul(out, hi[:, k], core.xn_hi[:, k], start=k == 0, stop=False)
        pe.matmul(out, hi[:, k], core.xn_lo[:, k], start=False, stop=False)
        ins = pe.matmul(out, lo[:, k], core.xn_hi[:, k], start=False, stop=k == KT - 1)
    ins.then_inc(done, 1)


def gate_weights(core, ctx):
    return [core.sb("gate_" + n, [P, KT, 96], d, ctx) for n, d in (("w", F32), ("w_hi", F32R), ("w_lo", F32R))]


def setup(nc, core, io, scr, gw):
    with ExitStack() as tmp:
        sb = lambda n, s, d=F32: core.sb(n, s, d, tmp)
        sem = lambda n: nc.alloc_semaphore(name="su_" + n)
        xr = sb("x_rows", [P, 3, D])
        xT = sb("su_xT", [P, KT, T])
        par = sb("par_rows", [P, 5, P])
        dsk = sb("d_skip", [32, 2])
        segw = sb("seg_wide", [P, 4, NB])
        sq, var, r, t1 = sb("su_sq", [P, 4, T]), sb("su_var", [P, T]), sb("su_r", [P, T]), sb("su_t", [P, T])
        x_in = [sem(f"x_in{q}") for q in range(4)]
        p_in, p_in_pool, made, dve_s, act_s, dex, tr, par_t = (
            sem(n) for n in ("par_in", "par_in_pool", "masks", "dve", "act", "d_wide", "x_turned", "par_turned"))
        ppar, msteps, gw_in, gw_hi, gw_lo, prod = (sem(n) for n in "par_pe pool gate_w_in gate_w_hi gate_w_lo product".split())
        norm = NormJob(core, sem, "norm", xT, C_NAB, sq, var, r, t1)
        block = tmp.enter_context(nc.Block())
        rows = lambda ap: ap.rearrange("o (t c) -> (o t) c", c=P)
        plan = [(rows(io["norm_ab"]), 0, 0), (rows(io["norm_c"]), 0, 16),
                (io["final_norm"].rearrange("(t c) -> t c", c=P), 0, 32), (rows(io["gla_norm"]), 0, 48),
                (rows(io["mlstm_norm"]), 0, 64), (rows(io["gla_b_a"]), 0, 80), (rows(io["mlstm_conv_b"]), 0, 88),
                (io["mlstm_conv_w"].rearrange("o k (t c) -> (o k t) c", c=P), 1, 0), (rows(io["ssd_norm"]), 1, 64),
                (io["ssd_conv_w"][:, 0:2].rearrange("o k (t c) -> (o k t) c", c=P), 2, 0),
                (io["ssd_conv_w"][:, 2:4].rearrange("o k (t c) -> (o k t) c", c=P), 3, 0),
                (rows(io["ssd_conv_b"]), 4, 0)]

        @block.sync
        def _(sp):
            for q in range(4):
                c = slice(q * D // 4, (q + 1) * D // 4)
                for j in range(2):
                    sp.dma_start(xr[:, j, c], io["x_prompt"][0, j * P:(j + 1) * P, c]).then_inc(x_in[q], 16)
                sp.dma_start(xr[0:TS, 2, c], io["x_sample"].rearrange("b t c -> (b t) c")[:, c]).then_inc(x_in[q], 16)
            for q in range(KT // 4):
                norm.store(sp, scr["x0T"], q)

        @block.gpsimd
        def _(pool):
            pool.memset(gw[0][:], 0.0).then_inc(msteps, 1)
            pool.memset(core.ident[:], 0.0)
            pool.memset(core.tri[:], 1.0)
            pool.memset(core.smask[:], 1.0)
            pool.memset(segw[:], 1.0).then_inc(msteps, 1)
            pool.wait_ge(msteps, 2)
            pool.affine_select(out=core.ident[:], in_=core.ident[:], compare_op=ALU.not_equal, fill=1.0,
                               base=0, pattern=[[-1, P]], channel_multiplier=1)
            pool.affine_select(out=core.tri[:], in_=core.tri[:], compare_op=ALU.is_ge, fill=0.0,
                               base=0, pattern=[[1, P]], channel_multiplier=-1)
            sm, sg = samples(core.smask[:]), segw[:]
            pool.affine_select(out=sm, in_=sm, compare_op=ALU.is_ge, fill=0.0, base=96,
                               pattern=[[TD, NB], [1, TD]], channel_multiplier=-1)
            pool.affine_select(out=sg, in_=sg, compare_op=ALU.is_ge, fill=0.0, base=0,
                               pattern=[[-TS, 4], [-TD, NB]], channel_multiplier=1).then_inc(msteps, 1)
            pool.wait_ge(msteps, 3)
            pool.affine_select(out=sm, in_=sm, compare_op=ALU.is_ge, fill=0.0, base=-96,
                               pattern=[[-TD, NB], [0, TD]], channel_multiplier=1)
            pool.affine_select(out=sg, in_=sg, compare_op=ALU.is_ge, fill=0.0, base=TD - 1,
                               pattern=[[TS, 4], [TD, NB]], channel_multiplier=-1).then_inc(made, 1)
            for src, slot, row in plan[6:]:
                pool.dma_start(par[row:row + src.shape[0], slot], src).then_inc(p_in_pool, 16)
            wv = io["w_in_ab"][0].rearrange("(k p) c -> p k c", p=P)
            for c, src, n in ((0, 6144, 16), (32, 14352, 4), (64, 14356, 4)):
                pool.dma_start(gw[0][:, :, c:c + n], wv[:, :, src:src + n]).then_inc(gw_in, 16)

        @block.vector
        def _(dve):
            st = Steps(dve, dve_s)
            dve.memset(core.ones[:], 1.0)
            st.then_wait(dve.memset(core.keep[:], 1.0))
            dve.memset(core.keep[:, 0:1], 0.0)
            dve.memset(samples(core.keep[:, S0:T])[:, :, 0:1], 0.0)
            for k in range(KT):
                dve.wait_ge(tr, k + 1)
                dve.tensor_copy(xT[:, k], core.bank[k % 4][:, 0:T]).then_inc(norm.ready, 1)
            dve.wait_ge(p_in, 16 * 7)
            dve.wait_ge(p_in_pool, 16 * (len(plan) - 6))
            dve.tensor_copy(par[96:128, 1].rearrange("p (two c) -> p two c", two=2),
                            dsk[:].unsqueeze(2).broadcast_to([32, 2, 64])).then_inc(dex, 1)
            dve.wait_ge(made, 1)
            for q in range(1, 4):
                st.then_wait(dve.tensor_tensor(segw[:, 0], segw[:, 0], segw[:, q], ALU.add))
            dve.tensor_copy(core.seg[:], segw[:, 0])
            for s, n in ((0, 104), (1, 128), (2, 96), (3, 96), (4, 48)):
                dve.wait_ge(ppar, s + 1)
                dve.tensor_copy(core.parT[:, s * P:s * P + n], core.bank[6 + s % 2][:, (s // 2) * P:(s // 2) * P + n]
                                ).then_inc(par_t, 1)
            dve.wait_ge(par_t, 5)
            dve.wait_ge(gw_hi, 1)
            dve.tensor_tensor(gw[2][:], gw[0][:], gw[1][:].bitcast(F32), ALU.subtract).then_inc(gw_lo, 1)
            norm.vector(dve, core.bank[4], st)
            dve.wait_ge(norm.done, KT // 4)

        @block.scalar
        def _(act):
            st = Steps(act, act_s)
            for src, slot, row in plan[:6]:
                act.dma_start(par[row:row + src.shape[0], slot], src).then_inc(p_in, 16)
            act.dma_start(dsk[:], io["ssd_d"].rearrange("o (t two) -> (o t) two", two=2)).then_inc(p_in, 16)
            for k in range(KT):
                norm.scalar_square(act, k, k + 1)
            act.wait_ge(gw_in, 48)
            act.activation(gw[1][:], gw[0][:], ACT.Copy).then_inc(gw_hi, 1)
            norm.scalar_r(act, st)

        @block.tensor
        def _(pe):
            pe.wait_ge(made, 1)
            for k in range(KT):
                if k % 4 == 0:
                    pe.wait_ge(x_in[k // 4], 48)
                if k >= 4:
                    pe.wait_ge(norm.ready, k - 3)
                c = slice(k * P, (k + 1) * P)
                b = core.bank[k % 4]
                pe.transpose(b[:, 0:P], xr[:, 0, c], core.ident[:])
                pe.transpose(b[:, P:2 * P], xr[:, 1, c], core.ident[:])
                pe.transpose(b[:, S0:T], xr[0:TS, 2, c], core.ident[0:TS, 0:TS]).then_inc(tr, 1)
                if k >= 3:
                    norm.tensor_sum(pe, core.bank[4], k - 3)
            for k in range(KT - 3, KT):
                norm.tensor_sum(pe, core.bank[4], k)
            pe.wait_ge(dex, 1)
            for s, n in ((0, 104), (1, 128), (2, 96), (3, 96), (4, 48)):
                if s >= 2:
                    pe.wait_ge(par_t, s - 1)
                pe.transpose(core.bank[6 + s % 2][:, (s // 2) * P:(s // 2) * P + n], par[0:n, s],
                             core.ident[0:n, 0:n]).then_inc(ppar, 1)
            pe.wait_ge(gw_lo, 1)
            gate_product(pe, core, gw[1], gw[2], core.bank[0][0:96, 0:T], norm.done, prod)


R_NM, R_EM, R_AL, R_M0, R_DEC, R_N = 0, T, 2 * T, 3 * T, 3 * T + TS, 3 * T + TS + NB


def layer0_buffers(core, ctx):
    sb = lambda n, s, d=F32: core.sb(n, s, d, ctx)
    return dict(hist=sb("ml_history", [P, 16, 24]),
                acol=sb("ml_a_cols", [P, 3, 4]), dcol=sb("ml_decay_cols", [NB, 4]),
                nrow=sb("ml_n_rows", [NB, 4 * DK]), nT=sb("ml_nT", [P, 8, NB]))


def gates0(nc, core, io, out, scr, g, ws):
    with ExitStack() as tmp:
        sb = lambda n, s, d=F32: core.sb(n, s, d, tmp)
        sem = lambda n: nc.alloc_semaphore(name="g0_" + n)
        wa = sb("w_a2", [16, 4 * DK])
        agT, au, mn = sb("agT", [16, T]), sb("abs_u", [P, 8, T]), sb("min_u", [P, 8, T])
        bif, m0 = sb("ml_bias", [4, 2]), sb("ml_m0", [4, NB])
        ir, fr, fa, fc, a, am, M, m, big = (sb("ml_" + n, [4, T]) for n in "i f fa fc a am M m big".split())
        gcum = sb("gla_gate_sum", [P, 8, T])
        apad, R, dex = sb("a_pad", [4, 384]), sb("ml_rows", [4, R_N]), sb("dec_exp", [4, NB])
        crow = sb("ml_conv_rows", [24, 2048])
        s_in, n_in, ag_d, gps, u_d, sp_d, fu_d, fl_d, dve_s, act_s, rows_d, dx_d, tps, gc_d, saved = (
            sem(n) for n in ("small_in n_in ag gate_psum u softplus "
                             "f_u f_softplus dve act rows decay turned gcum saved").split())
        block = tmp.enter_context(nc.Block())
        @block.sync
        def _(sp):
            sp.dma_start(wa[:], io["gla_w_a2"][0]).then_inc(s_in, 16)
            sp.dma_start(bif[:, 0:1], io["mlstm_b_i"].rearrange("o h -> h o")).then_inc(s_in, 16)
            sp.dma_start(bif[:, 1:2], io["mlstm_b_f"].rearrange("o h -> h o")).then_inc(s_in, 16)
            sp.dma_start(m0[:], io["state_mlstm_m"][0].rearrange("b h -> h b")).then_inc(s_in, 16)
            sp.dma_start(crow[:], io["state_mlstm_conv"][0].rearrange("b t c -> (b t) c")).then_inc(n_in, 16)
            sp.dma_start(g["nrow"][:], io["state_mlstm_n"][0].rearrange("b h k -> b (h k)")).then_inc(n_in, 16)
            wq = io["w_in_ab"][0].rearrange("(k p) c -> p k c", p=P)
            for j in range(UNITS):
                sp.dma_start(core.w_raw[:, j], wq[:, UK * j:UK * j + UK, 0:GW]).then_inc(ws["arrived"][j], 16)
            sp.wait_ge(rows_d, 1)
            sp.dma_start(scr["ml_rows"], R[:]).then_inc(saved, 16)
            sp.dma_start(out["mm_p"][0].rearrange("b h -> h b"), m[:, TP - 1:TP]).then_inc(saved, 16)
            sp.dma_start(out["mm_s"][0].rearrange("b h -> h b"),
                         samples(m[:, S0:T])[:, :, TD - 1]).then_inc(saved, 16)
            sp.wait_ge(gc_d, 8)
            sp.dma_start(scr["gcum"], gcum[:]).then_inc(saved, 16)
            sp.wait_ge(saved, 64)

        @block.scalar
        def _(act):
            st = Steps(act, act_s)
            act.wait_ge(fu_d, 1)
            st.then_wait(act.activation(fa[:], fr[:], ACT.Abs))
            st.then_wait(act.activation(fa[:], fa[:], ACT.Exp, scale=-1.0))
            act.activation(fa[:], fa[:], ACT.Ln, bias=1.0).then_inc(fl_d, 1)
            act.wait_ge(u_d, 8)
            st.then_wait(act.activation(au[:], mn[:], ACT.Abs))
            st.then_wait(act.activation(au[:], au[:], ACT.Exp, scale=-1.0))
            act.activation(au[:], au[:], ACT.Ln, bias=1.0).then_inc(sp_d, 1)
            act.wait_ge(rows_d, 1)
            act.activation(dex[:], R[:, R_DEC:R_N], ACT.Exp).then_inc(dx_d, 1)
            act.sem_inc(ws["used"], UNITS)
            split_hi(act, core, ws, 0)

        @block.tensor
        def _(pe):
            pe.wait_ge(ag_d, 1)
            pe.wait_ge(s_in, 64)
            for t in range(8):
                if t >= 4:
                    pe.wait_ge(u_d, t - 3)
                pe.matmul(core.bank[1 + t % 4][:, 0:T], wa[:, t * P:(t + 1) * P], agT[:], start=True, stop=True
                          ).then_inc(gps, 1)
            pe.wait_ge(n_in, 32)
            for t in range(16):
                pe.transpose(core.bank[5][:, 24 * t:24 * t + 24], crow[:, t * P:(t + 1) * P], core.ident[0:24, 0:24])
            for t in range(8):
                i = pe.transpose(core.bank[6][:, NB * t:NB * t + NB], g["nrow"][:, t * P:(t + 1) * P], core.ident[0:NB, 0:NB])
            i.then_inc(tps, 1)
            pe.wait_ge(dx_d, 1)
            for j in range(3):
                pe.transpose(core.bank[7][:, 4 * j:4 * j + 4], apad[:, j * P:(j + 1) * P], core.ident[0:4, 0:4])
            pe.transpose(core.bank[7][0:NB, 16:20], dex[:], core.ident[0:4, 0:4]).then_inc(tps, 1)

        @block.vector
        def _(dve):
            st = Steps(dve, dve_s)
            st.then_wait(dve.tensor_scalar(big[:], core.keep[0:4, :], 1.0, 3.0e38, ALU.subtract, ALU.mult))
            dve.tensor_copy(agT[:], core.bank[0][0:16, 0:T]).then_inc(ag_d, 1)
            dve.tensor_copy(ir[:], core.bank[0][32:36, 0:T])
            st.then_wait(dve.tensor_copy(fr[:], core.bank[0][64:68, 0:T]))
            dve.wait_ge(s_in, 64)
            dve.tensor_scalar(ir[:], ir[:], bif[:, 0:1], None, ALU.add)
            dve.tensor_scalar(fr[:], fr[:], bif[:, 1:2], None, ALU.add).then_inc(fu_d, 1)
            for t in range(8):
                b = core.bank[1 + t % 4][:, 0:T]
                ba = core.parT[:, C_BA + t:C_BA + t + 1]
                dve.wait_ge(gps, t + 1)
                dve.tensor_scalar(mn[:, t], b, ba, None, ALU.add).then_inc(u_d, 1)
            dve.wait_ge(fl_d, 1)
            st.then_wait(dve.scalar_tensor_tensor(fr[:], fr[:], 0.0, fa[:], ALU.min, ALU.subtract))
            st.then_wait(dve.tensor_tensor_scan(fc[:], core.keep[0:4, :], fr[:], 0.0, ALU.mult, ALU.add))
            dve.memset(apad[:, TP:384], 0.0)
            st.then_wait(dve.tensor_tensor(a[:], ir[:], fc[:], ALU.subtract))
            dve.tensor_copy(apad[:, 0:TP], a[:, 0:TP])
            dve.tensor_copy(apad[:, 352:384], a[:, S0:T])
            st.then_wait(dve.tensor_copy(am[:], a[:]))
            dve.tensor_scalar(am[:, 0:1], a[:, 0:1], 0.0, None, ALU.max)
            st.then_wait(dve.tensor_tensor(samples(am[:, S0:T])[:, :, 0], samples(a[:, S0:T])[:, :, 0], m0[:], ALU.max))
            st.then_wait(dve.tensor_tensor_scan(M[:], big[:], am[:], 0.0, ALU.add, ALU.max))
            st.then_wait(dve.tensor_tensor(m[:], fc[:], M[:], ALU.add))
            Ms = samples(M[:, S0:T])
            last = Ms[:, :, TD - 1:TD].broadcast_to([4, NB, TD])
            dve.tensor_scalar(R[:, R_NM:R_EM], M[:], -1.0, None, ALU.mult)
            dve.tensor_scalar(R[:, R_EM:R_AL], m[:], -1.0, None, ALU.mult)
            dve.tensor_scalar(R[:, R_AL:R_AL + TP], a[:, 0:TP], M[:, TP - 1:TP], None, ALU.subtract)
            dve.tensor_tensor(samples(R[:, R_AL + TP:R_M0]), samples(a[:, S0:T]), last, ALU.subtract)
            dve.tensor_tensor(samples(R[:, R_M0:R_DEC]), m0[:].unsqueeze(2).broadcast_to([4, NB, TD]), Ms, ALU.subtract)
            dve.tensor_tensor(R[:, R_DEC:R_N], m0[:], Ms[:, :, TD - 1], ALU.subtract).then_inc(rows_d, 1)
            dve.wait_ge(sp_d, 1)
            st.then_wait(dve.scalar_tensor_tensor(mn[:], mn[:], 0.0, au[:], ALU.min, ALU.subtract))
            for t in range(8):
                dve.tensor_tensor_scan(gcum[:, t], core.keep[:], mn[:, t], 0.0, ALU.mult, ALU.add).then_inc(gc_d, 1)
            dve.wait_ge(tps, 2)
            dve.tensor_copy(g["hist"][:].rearrange("p t c -> p (t c)"), core.bank[5][:, 0:384])
            dve.tensor_copy(g["nT"][:].rearrange("p t c -> p (t c)"), core.bank[6][:, 0:64])
            dve.tensor_copy(g["acol"][:].rearrange("p t c -> p (t c)"), core.bank[7][:, 0:12])
            st.then_wait(dve.tensor_copy(g["dcol"][:], core.bank[7][0:NB, 16:20]))
            dve.sem_inc(ws["split"], RAW)
            split_lo(dve, core, ws, 0)


G_QI, G_QR, G_QE, G_KI, G_KF, G_N = 0, T, T + 192, T + 224, T + 608, 2 * T + 608
UPD = 16


def ab_mixers(nc, core, io, out, scr, g, ws):
    with ExitStack() as tmp:
        sb = lambda n, s, d=F32: core.sb(n, s, d, tmp)
        sem = lambda n: nc.alloc_semaphore(name="ab_" + n)
        act_b = sb("proj", [P, 12, T])
        cq = sb("ml_qk_padded", [P, 4, 3 + TP + NB * 7])
        state = sb("state", [P, NB, 2, DV])
        DD = sb("factors", [P, 2, G_N])
        Ek = sb("k_factor", [P, 2, T])
        mlb = sb("head_rows", [P, R_N])
        gb = mlb[:, 0:2 * T].rearrange("p (k t) -> p k t", k=2)
        kf = sb("k_final", [P, 2, T])
        ks4, vs4 = sb("k_stack", [P, 2, P]), sb("v_stack", [P, 4, P])
        qe = sb("q_state", [P, 2, TS])
        qn = sb("q_n", [P, 2, TS])
        att = sb("att", [P, 416])
        Dm = att
        vrow, v3 = sb("v_rows", [P, 2, DV]), sb("v3", [96, DV], F32R)
        krow, k3m = sb("k_rows", [P, 2, DK]), sb("k3m", [96, NB, DK], F32R)
        room = sb("few_rows", [P, 1024])
        vs, kfull = room[:, 0:DV], room[:, DV:DV + DK]
        tailr, nout, npr = room[0:27, 0:512], room[0:NB, 512:768], room[0:1, 768:1024]
        CP = 3 + TP + NB * 7
        CL = CP - 3
        oT, wide = sb("oT", [P, 4, T]), sb("wide", [P, 2, 4, CP])
        sq, tz, cy, cth = wide[:, 0, :, 0:T], wide[:, 1, :, 0:T], wide[:, 0], wide[:, 1]
        var, r, t1 = (sb(n, [P, T]) for n in ("var", "r", "t1"))
        rden = t1
        pst = DD[:].rearrange("p k c -> p (k c)")[:, 0:2 * DV].rearrange("p (k v) -> p k v", k=2)
        dec = sb("decay", [P, 2, NB])
        wn, cw, ncur, acur = sb("norm_w", [P, 4]), sb("conv_w", [P, 4, 5]), sb("n_cur", [P, 2, NB]), sb("a_cur", [P, 3])
        tail = sb("conv_tail", [P, 4, 27])
        names = ("gb_in gb_used proj_free gates_taken qk_used e0 e_exp e_exps e_tanh ml_conv ml_rows_in ml_rows_used tail_rows tail_turned "
                 "tail_copied tail_out att att_done v_turned v_rows k_turned k_rows k_rest den den_read o_psum o_out o_sq rms var_ok r_first "
                 "pstate pstate_out pstate_stored n_psum n_done n_stored upd upd_done o_ready o_stored tanh_o arg dexp states state_rows q_wide "
                 "tanh_z dve act pool_w").split()
        s = {n: sem(n) for n in names}
        st_in = [sem(f"state_in{b}") for b in range(NB)]
        st_out = [sem(f"state_out{b}") for b in range(NB)]
        block = tmp.enter_context(nc.Block())
        B = core.bank
        proj_banks = [(B[0], B[1]), (B[2], B[3])]
        wv = io["w_in_ab"][0].rearrange("(k p) c -> p k c", p=P)
        NQ = 4 * 6 + 4 * 8

        def source(ml, h, gr):
            if not ml:
                return (h * DK, 1024 + h * DK, 2048 + h * DV, 2048 + GW + h * DV, 4096 + h * DV, 4096 + GW + h * DV)[gr]
            return 6160 + (h * DK, 1024 + h * DK, 2048 + h * DV, 2048 + GW + h * DV, 4096 + h * DV, 4096 + GW + h * DV,
                           6144 + h * DV, 6144 + GW + h * DV)[gr]

        def turns(eng):
            yield (0, 0, 0, None, None, None)
            with eng.Fori(1, 4) as h:
                yield (0, h, h * 6, 0, h - 1, h - 1)
            yield (1, 0, 24, 0, 3, 3)
            with eng.Fori(1, 4) as h:
                yield (1, h, h * 8 + 24, 1, h - 1, h + 3)
            yield (None, None, None, 1, 3, 7)

        wo = io["w_out_ab"][0].rearrange("(k p) c -> p k c", p=P)

        def load_head(sp, ml, h, q0, first=0):
            for gr in range(first, 8 if ml else 6):
                c0 = source(ml, h, gr)
                for j in range(UNITS):
                    load_unit(sp, core, ws, q0 + gr, j, wv[:, UK * j:UK * j + UK, bass.ds(c0, GW)])

        @block.sync
        def _(sp):
            load_head(sp, 0, 0, 0, first=1)
            with sp.Fori(1, 4) as h:
                load_head(sp, 0, h, h * 6)
            load_head(sp, 1, 0, 24)
            with sp.Fori(1, 4) as h:
                load_head(sp, 1, h, h * 8 + 24)
            for j in range(UNITS):
                load_unit(sp, core, ws, NQ, j, wo[:, UK * j:UK * j + UK, 0:GW])

        def pool_wait(pool, sm, value):
            pool.wait_ge(sm, value)
            pool.sem_inc(s["pool_w"], 1)

        sg_in, sg_out = io["state_gla"][0], out["gla_s"][0]
        sm_in, sm_out = io["state_mlstm_c"][0], out["mc_s"][0]
        tiles_of = lambda ap: ap.rearrange("o (k p) v -> p (o k) v", p=P)

        def load_state(pool, ml, h, H, b):
            src = (sm_in if ml else sg_in)[b, bass.ds(h, 1)]
            if not (isinstance(H, int) and H == 0):
                pool_wait(pool, st_out[b], H * 16)
            pool.dma_start(state[:, b], tiles_of(src)).then_inc(st_in[b], 16)

        def load_gates(pool, h):
            if not (isinstance(h, int) and h == 0):
                pool_wait(pool, s["gb_used"], h)
            pool.dma_start(gb, scr["gcum"][:, bass.ds(h * 2, 2), :]).then_inc(s["gb_in"], 16)

        def load_rows(pool, h):
            if isinstance(h, int) and h == 0:
                pool_wait(pool, s["gb_used"], 4)
            else:
                pool_wait(pool, s["ml_rows_used"], h)
            pool.dma_start(mlb[:], scr["ml_rows"][bass.ds(h, 1), :].partition_broadcast(P)).then_inc(s["ml_rows_in"], 16)

        def scan_dmas(pool, ml, h, H, next_state, next_rows=None):
            if ml:
                pool_wait(pool, s["tail_copied"], h + 1)
                for k, c0 in ((0, 0), (1, 1024)):
                    pool.dma_start(out["mcv_p"][0, 0][:, bass.ds(h * DK + c0, DK)], tailr[0:3, k * DK:(k + 1) * DK]
                                   ).then_inc(s["tail_out"], 16)
                    pool.dma_start(out["mcv_s"][0].rearrange("b t c -> (b t) c")[:, bass.ds(h * DK + c0, DK)],
                                   tailr[3:27, k * DK:(k + 1) * DK]).then_inc(s["tail_out"], 16)
            dst = out["mc_p" if ml else "gla_p"][0, 0]
            pool_wait(pool, s["pstate_out"], H + 1)
            pool.dma_start(dst[bass.ds(h, 1)].rearrange("o (k p) v -> p (o k) v", p=P), pst[:]).then_inc(s["pstate_stored"], 16)
            if ml:
                pool_wait(pool, s["n_done"], h + 1)
                pool.dma_start(out["mn_p"][0, 0][bass.ds(h, 1)], npr).then_inc(s["n_stored"], 16)
                pool.dma_start(out["mn_s"][0].rearrange("b h k -> b (h k)")[:, bass.ds(h * DK, DK)], nout
                               ).then_inc(s["n_stored"], 16)
            pool_wait(pool, s["o_ready"], H + 1)
            pool.dma_start(scr["oT"][:, bass.ds(H * 4, 4)], oT[:]).then_inc(s["o_stored"], 16)
            if next_rows is not None:
                load_rows(pool, next_rows)
            for b in range(NB):
                pool_wait(pool, s["upd_done"], H * UPD + (2 * b + 2 + 4))
                pool.dma_start(tiles_of((sm_out if ml else sg_out)[b, bass.ds(h, 1)]), state[:, b]).then_inc(st_out[b], 16)
            if next_state is not None:
                for b in range(NB):
                    load_state(pool, *next_state, H + 1, b)

        @block.gpsimd
        def _(pool):
            load_gates(pool, 0)
            for b in range(NB):
                load_state(pool, 0, 0, 0, b)
            with pool.Fori(0, 3) as h:
                load_gates(pool, h + 1)
                scan_dmas(pool, 0, h, h, (0, h + 1))
            load_rows(pool, 0)
            scan_dmas(pool, 0, 3, 3, (1, 0))
            with pool.Fori(0, 3) as h:
                scan_dmas(pool, 1, h, h + 4, (1, h + 1), h + 1)
            scan_dmas(pool, 1, 3, 7, None)
            for b in range(NB):
                pool_wait(pool, st_out[b], 16 * 8)
            pool_wait(pool, s["o_stored"], 16 * 8)
            pool_wait(pool, s["pstate_stored"], 16 * 8)
            pool_wait(pool, s["n_stored"], 32 * 4)
            pool_wait(pool, s["tail_out"], 64 * 4)

        def t_att(pe, ml, h, H):
            pe.wait_ge(s["e0"], H + 1)
            pe.wait_ge(s["upd_done"], H * UPD + 4)
            if not ml:
                blocks = [(64 * (c % 2), 64, (0, 64, 256, 320)[c], Ek, 64 * c, G_QI + 64 * c) for c in range(4)]
                blocks += [(0, 64, 64, DD, G_KI, G_QR), (0, 128, 128, DD, G_KI + 64, G_QR + 64),
                           (0, 128, 192, DD, G_KI + 192, G_QR + 128), (0, 64, 320, DD, G_KI + 320, G_QR + 128)]
                for row, n, col, kb, kc, qc in blocks:
                    for kt in range(2):
                        pe.matmul(B[4][row:row + n, col:col + 64], kb[:, kt, kc:kc + n], DD[:, kt, qc:qc + 64],
                                  start=kt == 0, stop=kt == 1)
                for kt in range(2):
                    i = pe.matmul(B[4][96:128, 384:416], Ek[:, kt, S0:T], DD[:, kt, G_QI + S0:G_QI + T],
                                  start=kt == 0, stop=kt == 1)
                i.then_inc(s["att"], 1)
            else:
                qv, kv = DD[:, :, 0:T], DD[:, :, T:2 * T]
                for row, n, c0, c1, i0, i1, j0 in ((0, 128, 0, 256, 0, 256, 0), (0, 128, 256, 384, 128, 256, 128),
                                                   (96, 32, 384, 416, S0, T, S0)):
                    for kt in range(2):
                        i = pe.matmul(B[4][row:row + n, c0:c1], kv[:, kt, j0:j0 + n], qv[:, kt, i0:i1],
                                      start=kt == 0, stop=kt == 1)
                i.then_inc(s["att"], 1)
            v0 = 0 if ml else 4
            for j in range(2):
                for f in range(4):
                    pe.transpose(B[5 + j][:, f * P:(f + 1) * P], act_b[:, v0 + f, j * P:(j + 1) * P], core.ident[:])
            if ml:
                pe.wait_ge(s["tail_copied"], h + 1)
            for f in range(4):
                i = pe.transpose(B[7][:, f * P:(f + 1) * P], vs4[:, f], core.ident[:])
            i.then_inc(s["v_turned"], 1)

        def t_krows(pe, ml, h, H):
            pe.wait_ge(s["v_rows"], H + 1)
            for j in range(2):
                for kt in range(2):
                    pe.transpose(B[5][:, (2 * j + kt) * P:(2 * j + kt + 1) * P], kf[:, kt, j * P:(j + 1) * P], core.ident[:])
            for kt in range(2):
                i = pe.transpose(B[6][:, kt * P:(kt + 1) * P], ks4[:, kt], core.ident[:])
            i.then_inc(s["k_turned"], 1)
            pe.wait_ge(s["att_done"], H + 1)
            if ml:
                mm = lambda *a, **k: pe.matmul(*a, skip_group_check=True, **k)
                mm(B[4][:, 0:256], core.ones[:], att[:, 0:256], start=True, stop=False)
                mm(B[4][:, 128:256], core.ones[:], att[:, 256:384], start=False, stop=False)
                mm(B[4][:, S0:T], core.ones[96:128, :], att[96:128, 384:416], start=False, stop=False)
                for kt in range(2):
                    i = mm(B[4][:, S0:T], core.ones[:], qn[:, kt], start=False, stop=kt == 1)
                i.then_inc(s["den"], 1)
            t_states(pe, ml, h, H)

        def q_wide(ml):
            v0 = 0 if ml else 4
            return act_b[:, v0:v0 + 2]

        def state_rows(ml):
            v0 = 2 if ml else 6
            return act_b[96:128, v0:v0 + 2].rearrange("p f t -> p (f t)")[:, 0:DV]

        def t_states(pe, ml, h, H):
            pe.wait_ge(s["q_wide"], H + 1)
            for b in range(NB):
                pe.wait_ge(st_in[b], H * 16 + 16)
                for kt in range(2):
                    i = pe.matmul(B[7][96:128, :], q_wide(ml)[:, kt, TS * b:TS * b + TS], state[:, b, kt],
                                  start=b == 0 and kt == 0, stop=b == NB - 1 and kt == 1)
            i.then_inc(s["states"], 1)

        def t_pv(pe, ml, h, H):
            pe.wait_ge(s["k_rows"], H + 1)
            if ml:
                pe.wait_ge(s["den_read"], h + 1)
            pe.wait_ge(s["state_rows"], H + 1)
            mm = lambda *a, **k: pe.matmul(*a, skip_group_check=True, **k)
            for f in range(4):
                bk, c = B[4 + f], slice(f * P, (f + 1) * P)
                mm(bk[:, 0:256], vrow[:, 0, c], att[:, 0:256], start=True, stop=False)
                mm(bk[:, 128:256], vrow[:, 1, c], att[:, 256:384], start=False, stop=False)
                mm(bk[:, S0:T], vs[96:128, c], att[96:128, 384:416], start=False, stop=False)
                mm(bk[:, S0:T], state_rows(ml)[:, c], core.ident[96:128, 96:128], start=False, stop=True).then_inc(s["o_psum"], 1)

        def t_rms(pe, ml, h, H):
            pe.wait_ge(s["o_out"], H * 4 + 4)
            for kt in range(2):
                for j in range(2):
                    i = pe.matmul(B[4 + kt][:, :], krow[:, j, kt * P:(kt + 1) * P], vrow[:, j, :], start=j == 0, stop=j == 1)
            i.then_inc(s["pstate"], 1)
            if ml:
                pe.matmul(B[7][0:1, 0:DK], core.ones[:, 0:1], krow[:, 0, :], start=True, stop=False)
                pe.matmul(B[7][0:1, 0:DK], core.ones[:, 0:1], krow[:, 1, :], start=False, stop=True)
                pe.matmul(B[7][0:NB, DK:2 * DK], core.seg[96:128, :], kfull[96:128, :], start=True, stop=True
                          ).then_inc(s["n_psum"], 1)
            pe.wait_ge(s["o_sq"], H + 1)
            for f in range(4):
                i = pe.matmul(B[6][:, 0:T], core.ones[:], sq[:, f], start=f == 0, stop=f == 3)
            i.then_inc(s["rms"], 1)

        def t_update(pe, ml, h, H, i0, i1):
            if i0 == 0:
                pe.wait_ge(s["pstate_out"], H + 1)
                pe.wait_ge(s["var_ok"], H + 1)
                if ml:
                    pe.wait_ge(s["n_done"], h + 1)
            for i in range(i0, i1):
                b, kt = i // 2, i % 2
                pe.wait_ge(s["upd_done"], H * UPD + (i + 1))
                pe.matmul(B[4 + i % 4][:, :], k3m[:, b, kt * P:(kt + 1) * P], v3[:], start=True, stop=True
                          ).then_inc(s["upd"], 1)

        def t_part(pe, slot, ml, h, H):
            first = (t_att, t_krows, t_pv, t_rms)
            first[slot](pe, ml, h, H)

        def t_tail(pe, h):
            pe.wait_ge(s["tail_rows"], h + 1)
            pe.wait_ge(s["upd_done"], (h + 4) * UPD + 4)
            for k in range(4):
                i = pe.transpose(B[7][0:27, k * P:(k + 1) * P], tail[:, k], core.ident[:])
            i.then_inc(s["tail_turned"], 1)

        @block.tensor
        def _(pe):
            for ml, h, q0, sml, sh, H in turns(pe):
                slots = 8 if ml or sml else 6
                for i in range(slots):
                    if ml is not None:
                        pe.wait_ge(s["proj_free"], q0 + i + 1)
                    for j in range(UNITS):
                        if ml is not None:
                            project_unit(pe, core, ws, q0 + i, j, core.xn_hi, core.xn_lo, 0, proj_banks[i % 2], True, True)
                        if sml is not None and 4 <= i < (8 if sml else 6):
                            n = UPD // ((4 if sml else 2) * UNITS)
                            u0 = ((i - 4) * UNITS + j) * n
                            t_update(pe, sml, sh, H, u0, u0 + n)
                    if sml is not None and i < 4:
                        if i == 0 and sml:
                            t_tail(pe, sh)
                        t_part(pe, i, sml, sh, H)

        def a_evac(act, ml, h, q0, i):
            H = h + (4 if ml else 0)
            act.wait_ge(ws["used"], (q0 + i) * UNITS + 2 * UNITS)
            hz = isinstance(h, int) and h == 0
            if i == 0 and not (hz and not ml):
                act.wait_ge(s["qk_used"], H)
            if i == 2 and not (hz and not ml):
                act.wait_ge(s["o_psum"], H * 4)
            if i == 4 and not (hz and not ml):
                act.wait_ge(s["o_ready"], H)
            for m in range(2):
                bk = proj_banks[i % 2][m]
                if ml and i < 2:
                    act.activation(cq[:, 2 * i + m, 3:3 + TP], bk[:, 0:TP], ACT.Copy)
                    ins = act.activation(samples(cq[:, 2 * i + m, 3 + TP:], 7)[:, :, 3:7], samples(bk[:, S0:T]), ACT.Copy)
                else:
                    ins = act.activation(act_b[:, (2 * i - (4 if ml else 0)) + m], bk[:, 0:T], ACT.Copy)
            ins.then_inc(s["proj_free"], 1)

        def a_e0(act, part, h, st):
            if part == "gla":
                act.wait_ge(s["gates_taken"], h + 1)
                st.then_wait(act.activation(Ek[:], DD[:, :, 0:T], ACT.Exp, scale=-1.0 / 16))
                act.activation(DD[:], DD[:], ACT.Exp, scale=1.0 / 16).then_inc(s["e_exp"], 1)
            if part == "conv":
                act.wait_ge(s["ml_conv"], h + 1)
                act.activation(cth[:, :, 0:CL], cy[:, :, 0:CL], ACT.Tanh).then_inc(s["e_tanh"], 1)
            if part == "exps":
                act.wait_ge(s["ml_rows_in"], h * 16 + 16)
                act.activation(mlb[:, R_EM:R_N], mlb[:, R_EM:R_N], ACT.Exp).then_inc(s["e_exps"], 1)
                act.wait_ge(s["arg"], h + 1)
                act.activation(Dm[:, 0:384], Dm[:, 0:384], ACT.Exp)
                act.activation(Dm[96:P, 384:416], Dm[96:P, 384:416], ACT.Exp).then_inc(s["dexp"], 1)

        def a_part(act, slot, ml, h, H, st):
            if slot == 0:
                act.wait_ge(s["proj_free"], (h * 8 + (24 + 8 + 2)) if ml else (h * 6 + (6 + 2)))
                act.wait_ge(s["v_turned"], H + 1)
                for j in range(2):
                    act.activation(vrow[:, j], B[5 + j][:, :], ACT.Copy)
                act.activation(v3[:], B[7][0:96, :], ACT.Copy)
                act.activation(vs[96:128], B[7][96:128, :], ACT.Copy).then_inc(s["v_rows"], 1)
                if ml:
                    act.wait_ge(s["o_ready"], H)
                    act.activation(sq, act_b[:, 4:8], ACT.Tanh, scale=0.5).then_inc(s["tanh_o"], 1)
                if not (isinstance(H, int) and H == 0):
                    act.wait_ge(s["o_ready"], H)
                act.activation(tz, act_b[:, 8:12], ACT.Tanh, scale=0.5).then_inc(s["tanh_z"], 1)
            if slot == 1:
                if ml:
                    act.wait_ge(s["den"], h + 1)
                    act.activation(rden[:], B[4][:, 0:T], ACT.Abs).then_inc(s["den_read"], 1)
                act.wait_ge(s["states"], H + 1)
                act.activation(state_rows(ml), B[7][96:128, :], ACT.Copy).then_inc(s["state_rows"], 1)
            if slot == 2:
                if not ml:
                    for f in range(4):
                        act.wait_ge(s["o_psum"], H * 4 + (f + 1))
                        if f == 0 and not (isinstance(H, int) and H == 0):
                            act.wait_ge(s["o_stored"], H * 16)
                        act.activation(oT[:, f], B[4 + f][:, 0:T], ACT.Copy).then_inc(s["o_out"], 1)
                    act.wait_ge(s["o_out"], H * 4 + 4)
                else:
                    act.wait_ge(s["k_rest"], h + 1)
                act.activation(sq, oT[:], ACT.Square).then_inc(s["o_sq"], 1)
            if slot == 3:
                act.wait_ge(s["pstate"], H + 1)
                if not (isinstance(H, int) and H == 0):
                    act.wait_ge(s["pstate_stored"], H * 16)
                act.activation(pst[:, 0], B[4][:, :], ACT.Copy)
                act.activation(pst[:, 1], B[5][:, :], ACT.Copy).then_inc(s["pstate_out"], 1)
                act.wait_ge(s["var_ok"], H + 1)
                rsqrt_act(act, r[:], var[:], st).then_inc(s["r_first"], 1)

        @block.scalar
        def _(act):
            st = Steps(act, s["act"])
            act.sem_inc(s["proj_free"], 2)
            for ml, h, q0, sml, sh, H in turns(act):
                st.restart()
                slots = 8 if ml or sml else 6
                for i in range(slots):
                    for j in range(UNITS):
                        if ml is not None:
                            split_hi_unit(act, core, ws, q0 + i + 1, j)
                        if ml == 0 and (i, j) == (4, 3):
                            a_e0(act, "gla", h, st)
                        if ml and (i, j) == (5, 0):
                            a_e0(act, "conv", h, st)
                        if ml and (i, j) == (5, 2):
                            a_e0(act, "exps", h, st)
                    if ml is not None:
                        a_evac(act, ml, h, q0, i)
                    if sml is not None and i < (8 if sml else 6):
                        a_part(act, i, sml, sh, H, st)
                if ml == 0:
                    act.wait_ge(s["upd_done"], h * UPD + 4)
                    act.activation(dec[:], samples2(gb[:, :, S0:T])[:, :, :, TD - 1], ACT.Exp, scale=1.0 / 16
                                   ).then_inc(s["gb_used"], 1)

        def v_gla_differences(dve, h):
            dve.wait_ge(s["gb_in"], h * 16 + 16)
            if not (isinstance(h, int) and h == 0):
                dve.wait_ge(s["pstate_stored"], h * 16)
            for kt in range(2):
                c4 = lambda ap: ap.rearrange("p (c t) -> p c t", t=CH)
                sub = lambda o, a_, b_: dve.tensor_tensor(o, a_, b_, ALU.subtract)
                gk, D1 = gb[:, kt], DD[:, kt]
                sub(c4(D1[:, 0:TP]), c4(gk[:, 0:TP]), c4(gk[:, 0:TP])[:, :, CH // 2:CH // 2 + 1].broadcast_to([P, 4, CH]))
                gs1 = samples(gk[:, S0:T])
                sub(samples(D1[:, S0:T]), gs1, gs1[:, :, TD // 2:TD // 2 + 1].broadcast_to([P, NB, TD]))
                sub(c4(D1[:, G_QR:G_QR + 192]), c4(gk[:, CH:TP]), c4(gk[:, 0:192])[:, :, CH - 1:CH].broadcast_to([P, 3, CH]))
                dve.tensor_copy(D1[:, G_QE:G_QE + TS], gk[:, S0:T])
                o = G_KI
                for c in range(1, 4):
                    sub(D1[:, o:o + CH * c], gk[:, CH * c - 1:CH * c].broadcast_to([P, CH * c]), gk[:, 0:CH * c])
                    o += CH * c
                sub(D1[:, G_KF:G_KF + TP], gk[:, TP - 1:TP].broadcast_to([P, TP]), gk[:, 0:TP])
                ins = sub(samples(D1[:, G_KF + TP:G_N]), gs1[:, :, TD - 1:TD].broadcast_to([P, NB, TD]), gs1)
            ins.then_inc(s["gates_taken"], 1)

        def v_gla_factors(dve, h, st):
            dve.wait_ge(s["proj_free"], h * 6 + (4 + 2))
            dve.wait_ge(s["e_exp"], h + 1)
            q, k = act_b[:, 0:2], act_b[:, 2:4]
            prod = lambda c0, n, x: dve.tensor_tensor(DD[:, :, c0:c0 + n], DD[:, :, c0:c0 + n], x, ALU.mult)
            qprod = lambda c0, n, x: dve.scalar_tensor_tensor(DD[:, :, c0:c0 + n], DD[:, :, c0:c0 + n], DK ** -0.5, x,
                                                              ALU.mult, ALU.mult)
            qprod(G_QI, T, q)
            qprod(G_QR, 192, q[:, :, CH:TP])
            dve.scalar_tensor_tensor(qe[:], DD[:, :, G_QE:G_QE + TS], DK ** -0.5, q[:, :, S0:T], ALU.mult, ALU.mult)
            dve.tensor_tensor(Ek[:], Ek[:], k, ALU.mult)
            o = G_KI
            for c in range(1, 4):
                prod(o, CH * c, k[:, :, 0:CH * c])
                o += CH * c
            st.then_wait(dve.tensor_tensor(kf[:], DD[:, :, G_KF:G_N], k, ALU.mult))

        def v_stacks(dve, ml, h, H, st):
            for stack, x, order in ((ks4, kf[:, :, S0:T], (0, 0, 1)), (vs4, act_b[:, (0 if ml else 4):(4 if ml else 8), S0:T], (0, 1, 0))):
                r4 = stack[:].bitcast(F32R)
                for i, o in enumerate(order):
                    if o == 0:
                        dve.tensor_copy(r4[:, :, TS * i:TS * i + TS], x)
                st.then_wait(dve.tensor_copy(stack[:, :, 96:128], x))
                i = order.index(1)
                st.then_wait(dve.tensor_tensor(r4[:, :, TS * i:TS * i + TS], x, stack[:, :, 0:TS], ALU.subtract))

        def v_ml_start(dve, h, st):
            dve.wait_ge(s["proj_free"], h * 8 + (24 + 2 + 2))
            dve.wait_ge(s["o_ready"], h + 4)
            for k in range(2):
                for m in range(2):
                    hv = samples(cq[:, 2 * k + m, 3 + TP:], 7)[:, :, 0:3]
                    dve.tensor_copy(hv, g["hist"][:, bass.ds(h * 2 + (8 * k + m), 1), :].rearrange("p o (b t) -> p (o b) t", t=3))
                for tap in range(4):
                    dve.tensor_scalar(cw[:, 2 * k:2 * k + 2, tap], core.parT[:, bass.ds(h * 2 + (C_MCW + 16 * tap + 8 * k), 2)],
                                      0.5, None, ALU.mult)
                dve.tensor_scalar(cw[:, 2 * k:2 * k + 2, 4], core.parT[:, bass.ds(h * 2 + (C_MCB + 8 * k), 2)], 0.5, None, ALU.mult)
            st.then_wait(dve.tensor_copy(ncur[:], g["nT"][:, bass.ds(h * 2, 2), :]))
            st.then_wait(dve.tensor_copy(acur[:], g["acol"][:, :, bass.ds(h, 1)].rearrange("p j o -> p (j o)")))
            if not (isinstance(h, int) and h == 0):
                dve.wait_ge(s["tail_turned"], h)
            for m in range(4):
                dve.tensor_copy(tail[:, m, 0:3], cq[:, m, TP:TP + 3])
                ins = dve.tensor_copy(tail[:, m, 3:27].rearrange("p (b t) -> p b t", t=3), samples(cq[:, m, 3 + TP:], 7)[:, :, 4:7])
            ins.then_inc(s["tail_rows"], 1)

        def v_ml_tap(dve, tap, st):
            for m in range(4):
                x, w_ = cq[:, m, tap:tap + CL], cw[:, m, tap:tap + 1]
                if tap == 0:
                    ins = dve.tensor_scalar(cy[:, m, 0:CL], x, w_, cw[:, m, 4:5], ALU.mult, ALU.add)
                else:
                    ins = dve.scalar_tensor_tensor(cy[:, m, 0:CL], x, w_, cy[:, m, 0:CL], ALU.mult, ALU.add)
            if tap < 3:
                st.then_wait(ins)
            else:
                ins.then_inc(s["ml_conv"], 1)

        def v_ml_args(dve, h):
            dve.wait_ge(s["ml_rows_in"], h * 16 + 16)
            dve.wait_ge(s["o_out"], h * 4 + 16)
            for c0, c1, i0, rows, j in ((0, 256, 0, slice(0, P), 0), (256, 384, 128, slice(0, P), 1), (384, 416, S0, slice(96, P), 2)):
                ins = dve.tensor_scalar(Dm[rows, c0:c1], mlb[rows, R_NM + i0:R_NM + i0 + c1 - c0], acur[rows, j:j + 1], 0.0,
                                        ALU.add, ALU.min)
            ins.then_inc(s["arg"], 1)

        def v_ml_silu(dve, h, st):
            dve.wait_ge(s["e_tanh"], h + 1)
            dve.wait_ge(s["pstate_stored"], h * 16 + 64)
            st.then_wait(dve.tensor_scalar(cy[:, 2:4, 0:CL], cy[:, 2:4, 0:CL], DK ** -0.5, None, ALU.mult))
            for m in range(4):
                o = DD[:, m % 2, (m // 2) * T:(m // 2) * T + T]
                dve.scalar_tensor_tensor(o[:, 0:TP], cth[:, m, 0:TP], 1.0, cy[:, m, 0:TP], ALU.add, ALU.mult)
                v7 = lambda x: samples(x[:, m, 3 + TP:CP], 7)[:, :, 0:TD]
                ins = dve.scalar_tensor_tensor(samples(o[:, S0:T]), v7(cth), 1.0, v7(cy), ALU.add, ALU.mult)
            st.then_wait(ins)

        def v_ml_factors(dve, h, st):
            dve.wait_ge(s["proj_free"], h * 8 + (24 + 4 + 2))
            dve.wait_ge(s["e_exps"], h + 1)
            qv, kv = DD[:, :, 0:T], DD[:, :, T:2 * T]
            dve.tensor_tensor(kf[:], kv, mlb[:, R_AL:R_M0].unsqueeze(1).broadcast_to([P, 2, T]), ALU.mult)
            st.then_wait(dve.tensor_tensor(qe[:], qv[:, :, S0:T], mlb[:, R_M0:R_DEC].unsqueeze(1).broadcast_to([P, 2, TS]), ALU.mult))
            for kt in range(2):
                dve.tensor_tensor(samples(qn[:, kt]), samples(qe[:, kt]), ncur[:, kt].unsqueeze(2).broadcast_to([P, NB, TD]), ALU.mult)

        def v_ml_mask(dve, h, st):
            dve.wait_ge(s["dexp"], h + 1)
            dve.tensor_tensor(Dm[:, 0:P], Dm[:, 0:P], core.tri[:], ALU.mult)
            dve.tensor_tensor(Dm[:, 256:384], Dm[:, 256:384], core.tri[:], ALU.mult)
            st.then_wait(dve.tensor_tensor(Dm[96:P, 384:416], Dm[96:P, 384:416], core.smask[96:P], ALU.mult))

        def v_part(dve, slot, ml, h, H, st):
            if slot == 0:
                if ml:
                    dve.wait_ge(s["tail_turned"], h + 1)
                    if not (isinstance(h, int) and h == 0):
                        dve.wait_ge(s["tail_out"], h * 64)
                    dve.tensor_copy(tailr, B[7][0:27, :]).then_inc(s["tail_copied"], 1)
                dve.wait_ge(s["att"], H + 1)
                if ml:
                    dve.tensor_tensor(att[:, 0:384], B[4][:, 0:384], Dm[:, 0:384], ALU.mult)
                    dve.tensor_tensor(att[96:P, 384:416], B[4][96:P, 384:416], Dm[96:P, 384:416], ALU.mult).then_inc(s["att_done"], 1)
                else:
                    dve.tensor_copy(att[0:64, 64:128], B[4][0:64, 64:128])
                    dve.tensor_copy(att[:, 128:256], B[4][:, 128:256])
                    dve.tensor_copy(att[0:64, 320:384], B[4][0:64, 320:384])
                    tri = core.tri[:].bitcast(U32)
                    for c, col in enumerate((0, 64, 256, 320)):
                        rows = slice(64 * (c % 2), 64 * (c % 2) + 64)
                        dve.copy_predicated(att[rows, col:col + CH], tri[rows, rows], B[4][rows, col:col + CH])
                    dve.copy_predicated(att[96:P, 384:416], core.smask[96:P].bitcast(U32), B[4][96:P, 384:416]
                                        ).then_inc(s["att_done"], 1)
                dve.wait_ge(s["v_turned"], H + 1)
                st.then_wait(dve.memset(q_wide(ml), 0.0))
                dve.tensor_copy(q_wide(ml).rearrange("p k (b s) -> p k b s", s=TS + TD)[:, :, :, 0:TD], samples2(qe[:])
                                ).then_inc(s["q_wide"], 1)
                c0 = C_MN if ml else C_GN
                st.then_wait(dve.tensor_scalar(wn[:], core.parT[:, bass.ds(h * 4 + c0, 4)], 0.5, None, ALU.mult))
            if slot == 1:
                dve.wait_ge(s["k_turned"], H + 1)
                dve.tensor_copy(krow[:].rearrange("p j c -> p (j c)"), B[5][:, :])
                if ml:
                    dve.tensor_copy(kfull[96:P, :], B[6][96:P, 0:DK])
                dve.tensor_tensor(k3m[:], B[6][0:96, 0:DK].unsqueeze(1).broadcast_to([96, NB, DK]),
                                  core.seg[0:96].unsqueeze(2).broadcast_to([96, NB, DK]), ALU.mult).then_inc(s["k_rows"], 1)
                if ml:
                    dve.wait_ge(s["den_read"], h + 1)
                    st.then_wait(dve.tensor_tensor(rden[:], rden[:], mlb[:, R_EM:R_AL], ALU.max))
                    st.then_wait(dve.reciprocal(rden[:], rden[:]))
                    st.then_wait(dve.tensor_scalar(rden[:], rden[:], 0.5, None, ALU.mult))
                    dve.sem_inc(s["ml_rows_used"], 1)
            if slot == 2 and ml:
                dve.wait_ge(s["tanh_o"], h + 1)
                dve.wait_ge(s["o_stored"], H * 16)
                for f in range(4):
                    dve.wait_ge(s["o_psum"], H * 4 + (f + 1))
                    dve.tensor_tensor(oT[:, f], B[4 + f][:, 0:T], rden[:], ALU.mult).then_inc(s["o_out"], 1)
                dve.wait_ge(s["o_out"], H * 4 + 4)
                dve.scalar_tensor_tensor(oT[:], sq, 1.0, oT[:], ALU.add, ALU.mult).then_inc(s["k_rest"], 1)
            if slot == 3:
                dve.wait_ge(s["rms"], H + 1)
                dve.tensor_scalar(var[:], B[6][:, 0:T], 1.0 / DV, EPS, ALU.mult, ALU.add).then_inc(s["var_ok"], 1)
                dve.wait_ge(s["tanh_z"], H + 1)
                dve.scalar_tensor_tensor(tz, tz, 1.0, act_b[:, 8:12], ALU.add, ALU.mult)
                if ml:
                    dve.wait_ge(s["n_psum"], h + 1)
                    if not (isinstance(h, int) and h == 0):
                        dve.wait_ge(s["n_stored"], h * 32)
                    dve.tensor_copy(npr, B[7][0:1, 0:DK])
                    dve.scalar_tensor_tensor(nout, g["nrow"][:, bass.ds(h * DK, DK)], g["dcol"][:, bass.ds(h, 1)],
                                             B[7][0:NB, DK:2 * DK], ALU.mult, ALU.add).then_inc(s["n_done"], 1)
                dve.wait_ge(s["r_first"], H + 1)
                st.then_wait(rsqrt_newton(dve, r[:], var[:], t1[:], st))
                for f in range(4):
                    ins = dve.scalar_tensor_tensor(oT[:, f], oT[:, f], wn[:, f:f + 1], r[:], ALU.mult, ALU.mult)
                st.then_wait(ins)
                dve.tensor_tensor(oT[:], oT[:], tz, ALU.mult).then_inc(s["o_ready"], 1)

        def v_update(dve, H, i0, i1):
            for i in range(i0, i1):
                b, kt = i // 2, i % 2
                dve.wait_ge(s["upd"], H * UPD + (i + 1))
                dve.scalar_tensor_tensor(state[:, b, kt], state[:, b, kt], dec[:, kt, b:b + 1], B[4 + i % 4][:, :],
                                         ALU.mult, ALU.add).then_inc(s["upd_done"], 1)

        @block.vector
        def _(dve):
            st = Steps(dve, s["dve"])
            dve.sem_inc(s["upd_done"], 4)
            dve.memset(att[:], 0.0)
            st.then_wait(dve.memset(cq[:, :, 0:3], 0.0))
            for ml, h, q0, sml, sh, H in turns(dve):
                st.restart()
                for i in range(8 if ml or sml else 6):
                    for j in range(UNITS):
                        if ml is not None:
                            split_lo_unit(dve, core, ws, q0 + i + 1, j)
                        if sml is not None and 4 <= i < (8 if sml else 6):
                            n = UPD // ((4 if sml else 2) * UNITS)
                            u0 = ((i - 4) * UNITS + j) * n
                            v_update(dve, H, u0, u0 + n)
                        if ml == 0 and (i, j) == (4, 1):
                            v_gla_differences(dve, h)
                        if ml == 0 and (i, j) == (5, 1):
                            v_gla_factors(dve, h, st)
                        if ml == 0 and (i, j) == (5, 2):
                            v_stacks(dve, ml, h, h, st)
                        if ml and i == 4:
                            if j == 0:
                                v_ml_start(dve, h, st)
                            v_ml_tap(dve, j, st)
                        if ml and (i, j) == (5, 0):
                            v_ml_args(dve, h)
                        if ml and (i, j) == (5, 2):
                            v_ml_silu(dve, h, st)
                        if ml and (i, j) == (6, 1):
                            v_ml_factors(dve, h, st)
                        if ml and (i, j) == (6, 2):
                            v_ml_mask(dve, h, st)
                        if ml and (i, j) == (6, 3):
                            v_stacks(dve, ml, h, h + 4, st)
                    if sml is not None and i < 4:
                        v_part(dve, i, sml, sh, H, st)
                if ml is not None:
                    dve.sem_inc(s["qk_used"], 1)
                    dve.sem_inc(s["e0"], 1)
                if ml:
                    dve.wait_ge(s["upd_done"], h * UPD + (4 * UPD + 4))
                    st.then_wait(dve.tensor_copy(dec[:], mlb[:, R_DEC:R_N].unsqueeze(1).broadcast_to([P, 2, NB])))
                if ml == 0:
                    dve.wait_ge(s["gb_used"], h + 1)


Q_OUT_AB, Q_SSD, Q_OUT_C = 56, 72, 112
OG = D // GW


def out_proj(nc, core, io, out, scr, ws, last, gw=None):
    tag = "oc" if last else "oa"
    q0 = Q_OUT_C if last else Q_OUT_AB
    w = io["w_out_c" if last else "w_out_ab"][0].rearrange("(k p) c -> p k c", p=P)
    with ExitStack() as tmp:
        sb = lambda n, s, d=F32: core.sb(f"{tag}_{n}", s, d, tmp)
        sem = lambda n: nc.alloc_semaphore(name=f"{tag}_{n}")
        o_hi, o_lo, o_raw = sb("o_hi", [P, 32, T], F32R), sb("o_lo", [P, 32, T], F32R), sb("o_raw", [P, 2, 4, T])
        xT, sq = sb("xT", [P, KT, T]), sb("sq", [P, 4, T])
        var, r, t1 = (sb(n, [P, T]) for n in ("var", "r", "t1"))
        RS = 4
        rows = o_raw[:].rearrange("p s k t -> p (s k t)")[:, 0:RS * 512].rearrange("p (s c) -> p s c", c=512)
        saved = [sem(f"saved{i}") for i in range(RS)]
        x_in, o_hi_d, o_split, dve_s, act_s, turned = (
            sem(n) for n in "x_in o_high o_split dve act turned".split())
        y_rows = [sem("y_rows_vector"), sem("y_rows_scalar")]
        gw_in, gw_hi, gw_lo, prod = (sem(n) for n in "gate_w_in gate_w_hi gate_w_lo product".split())
        wh, wl = (x[:].rearrange("p k t -> p (k t)")[:, 0:KT * 64].rearrange("p (k c) -> p k c", c=64) for x in (o_hi, o_lo))
        o_in = [sem(f"o_in{i}") for i in range(8)]
        norm = NormJob(core, sem, "norm", xT, C_FN if last else C_NC, sq, var, r, t1, xT if last else None)
        block = tmp.enter_context(nc.Block())
        B = core.bank
        pairs = [(B[0], B[1]), (B[2], B[3])]
        raw = lambda c: xT[:, 4 * c:4 * c + 4] if c < 4 else o_raw[:, c % 2]

        def load_quad(sp, q, og, half):
            for j in range(UNITS):
                k = KT * half + UK * j
                load_unit(sp, core, ws, q, j, w[:, k:k + UK, bass.ds(og * GW, GW)])

        @block.sync
        def _(sp):
            for c in range(6):
                sp.dma_start(raw(c), scr["oT"][:, 4 * c:4 * c + 4]).then_inc(o_in[c], 16)
            load_quad(sp, q0 + 1, 0, 1)
            with sp.Fori(1, OG) as og:
                for half in range(2):
                    load_quad(sp, og * 2 + (q0 + half), og, half)
            if last:
                for f in range(4):
                    for j in range(3):
                        n = 3 * f + j
                        sp.wait_ge(y_rows[n % 2], n // 2 + 1)
                        if j < 2:
                            sp.dma_start(out["y_p"][0, j * P:(j + 1) * P, f * 512:(f + 1) * 512], rows[:, n % RS]
                                         ).then_inc(saved[n % RS], 16)
                        else:
                            sp.dma_start(out["y_s"].rearrange("b t c -> (b t) c")[:, f * 512:(f + 1) * 512], rows[0:TS, n % RS]
                                         ).then_inc(saved[n % RS], 16)
                for i in range(RS):
                    sp.wait_ge(saved[i], 16 * 12 // RS)
            else:
                for q in range(3):
                    norm.store(sp, scr["x1T"], q)
                wc = io["w_in_c"][0].rearrange("(k p) c -> p k c", p=P)
                for j in range(UNITS):
                    load_unit(sp, core, ws, Q_SSD, j, wc[:, UK * j:UK * j + UK, 4096:4096 + GW])
                norm.store(sp, scr["x1T"], 3)

        @block.gpsimd
        def _(pool):
            for c in (6, 7):
                pool.wait_ge(o_split, c - 1)
                pool.dma_start(raw(c), scr["oT"][:, 4 * c:4 * c + 4]).then_inc(o_in[c], 16)
            pool.dma_start(xT[:], scr["x1T" if last else "x0T"]).then_inc(x_in, 16)
            if gw is not None:
                pool.dma_start(gw[:], io["w_in_c"][0].rearrange("(k p) c -> p k c", p=P)[:, :, 10240:10304]).then_inc(gw_in, 16)
                pool.wait_ge(gw_in, 16)

        def t_sums(pe, ks, n):
            for i, k in enumerate(ks):
                pe.wait_ge(norm.squared, n + i + 1)
                pe.matmul(B[4][:, 0:T], core.ones[:], sq[:, k], start=isinstance(n, int) and n + i == 0,
                          stop=isinstance(n, int) and n + i == KT - 1, skip_group_check=True).then_inc(norm.sq_free, 1)

        def t_group(pe, og, par, chunks=False):
            if not (isinstance(og, int) and og < 2):
                pe.wait_ge(norm.ready, og * 2 - 2)
            for half in range(2):
                for j in range(UNITS):
                    if chunks:
                        pe.wait_ge(o_split, UNITS * half + j + 1)
                    project_unit(pe, core, ws, og * 2 + (q0 + half), j, o_hi, o_lo, KT * half, pairs[par], half == 0, half == 1)

        @block.tensor
        def _(pe):
            t_group(pe, 0, 0, True)
            t_group(pe, 1, 1)
            t_sums(pe, (0, 1), 0)
            with pe.Fori(1, OG // 2) as pr:
                t_group(pe, pr * 2, 0)
                t_sums(pe, (2, 3), pr * 4 - 2)
                t_group(pe, pr * 2 + 1, 1)
                t_sums(pe, (0, 1), pr * 4)
            t_sums(pe, (2, 3), KT - 2)
            if gw is not None:
                pe.wait_ge(gw_lo, 1)
                gate_product(pe, core, wh, wl, B[0][0:64, 0:T], norm.done, prod)
            if last:
                for f in range(4):
                    pe.wait_ge(norm.done, 4 * f + 4)
                    for j in range(3):
                        n = 3 * f + j
                        if n >= 3:
                            pe.wait_ge(y_rows[(n - 3) % 2], (n - 3) // 2 + 1)
                        for m in range(4):
                            w_ = P if j < 2 else TS
                            i = pe.transpose(B[5 + n % 3][0:w_, m * P:(m + 1) * P], xT[:, 4 * f + m, j * P:j * P + w_], core.ident[:])
                        i.then_inc(turned, 1)

        def rows_out(eng, copy, n):
            k = P if n % 3 < 2 else TS
            eng.wait_ge(turned, n + 1)
            if n >= RS:
                eng.wait_ge(saved[n % RS], 16 * (n // RS))
            copy(rows[0:k, n % RS], B[5 + n % 3][0:k, :]).then_inc(y_rows[n % 2], 1)

        def a_squares(act, tiles, n):
            for i in range(2):
                if not (isinstance(n, int) and n < 4):
                    act.wait_ge(norm.sq_free, n + i - 3)
                act.wait_ge(norm.ready, n + i + 1)
                slot = (n + i) % 4 if isinstance(n, int) else tiles[1] + i
                act.activation(sq[:, slot:slot + 1], xT[:, bass.ds(n + i, 1)], ACT.Square).then_inc(norm.squared, 1)

        @block.scalar
        def _(act):
            st = Steps(act, act_s)
            for c in range(8):
                act.wait_ge(o_in[c], 16)
                act.activation(o_hi[:, 4 * c:4 * c + 4], raw(c), ACT.Copy).then_inc(o_hi_d, 1)
            for og in range(2):
                split_hi(act, core, ws, q0 + 2 * og + 1)
                split_hi(act, core, ws, q0 + 2 * og + 2)
                a_squares(act, None, 2 * og)
            with act.Fori(1, OG // 2 - 1) as pr:
                for par in range(2):
                    split_hi(act, core, ws, pr * 4 + (q0 + 2 * par + 1))
                    split_hi(act, core, ws, pr * 4 + (q0 + 2 * par + 2))
                    a_squares(act, (None, 2 * par), pr * 4 + 2 * par)
            for og in (OG - 2, OG - 1):
                split_hi(act, core, ws, q0 + 2 * og + 1)
                if not (last and og == OG - 1):
                    split_hi(act, core, ws, q0 + 2 * og + 2)
                a_squares(act, None, 2 * og)
            if gw is not None:
                act.wait_ge(gw_in, 16)
                act.activation(wh, gw[:], ACT.Copy).then_inc(gw_hi, 1)
            norm.scalar_r(act, st)
            if last:
                for n in range(1, 12, 2):
                    rows_out(act, lambda o, i: act.activation(o, i, ACT.Copy), n)

        def v_group(dve, og, par):
            dve.wait_ge(ws["used"], og * (2 * UNITS) + (q0 * UNITS + 3 * UNITS))
            for m in range(2):
                x = xT[:, bass.ds(og * 2 + m, 1)].rearrange("p o t -> p (o t)")
                dve.tensor_tensor(x, pairs[par][m][:, 0:T], x, ALU.add).then_inc(norm.ready, 1)

        @block.vector
        def _(dve):
            st = Steps(dve, dve_s)
            for c in range(8):
                dve.wait_ge(o_hi_d, c + 1)
                dve.tensor_tensor(o_lo[:, 4 * c:4 * c + 4], raw(c), o_hi[:, 4 * c:4 * c + 4].bitcast(F32),
                                  ALU.subtract).then_inc(o_split, 1)
            for og in range(2):
                split_lo(dve, core, ws, q0 + 2 * og + 1)
                split_lo(dve, core, ws, q0 + 2 * og + 2)
                if og == 0:
                    dve.wait_ge(x_in, 16)
                v_group(dve, og, og)
            with dve.Fori(1, OG // 2 - 1) as pr:
                for par in range(2):
                    split_lo(dve, core, ws, pr * 4 + (q0 + 2 * par + 1))
                    split_lo(dve, core, ws, pr * 4 + (q0 + 2 * par + 2))
                    v_group(dve, pr * 2 + par, par)
            for og in (OG - 2, OG - 1):
                split_lo(dve, core, ws, q0 + 2 * og + 1)
                if not (last and og == OG - 1):
                    split_lo(dve, core, ws, q0 + 2 * og + 2)
                v_group(dve, og, og % 2)
            if gw is not None:
                dve.wait_ge(gw_hi, 1)
                dve.tensor_tensor(wl, gw[:], wh.bitcast(F32), ALU.subtract).then_inc(gw_lo, 1)
            norm.vector(dve, B[4], st)
            dve.wait_ge(norm.done, KT if last else KT // 4)
            if last:
                for n in range(0, 12, 2):
                    rows_out(dve, dve.tensor_copy, n)


K_C0, K_C1, K_CS, K_C01, K_D0, K_D1, K_DS, K_W0, K_W1, K_N = range(10)


def layer1_buffers(core, ctx):
    return dict(hist=core.sb("ssd_history", [P, CT, 24], F32, ctx), cols=core.sb("ssd_cols", [P, K_N, SSD_H], F32, ctx))


def gates1(nc, core, io, scr, g):
    with ExitStack() as tmp:
        sb = lambda n, s, d=F32: core.sb("g1_" + n, s, d, tmp)
        sem = lambda n: nc.alloc_semaphore(name="g1_" + n)
        crow = sb("conv_rows", [24, 6144])
        par = sb("params", [64, 2])
        dt, au, c, keep2, wx = (sb(n, [64, T]) for n in "dt au c keep wexp".split())
        pad, we = sb("pad", [64, K_N * P]), sb("we", [64, 2 * TS])
        tot = sb("total", [64, 1])
        s_in, r_in, u_d, sp_d, wx_d, wx_e, pad_d, turned, dve_s, act_s, saved, nc_d = (
            sem(n) for n in "small_in rows_in u softplus w_arg w_exp pad turned dve act saved negc".split())
        block = tmp.enter_context(nc.Block())
        negc = au

        @block.sync
        def _(sp):
            sp.dma_start(par[:, 0:1], io["ssd_dt_bias"].rearrange("o h -> h o")).then_inc(s_in, 16)
            sp.dma_start(par[:, 1:2], io["ssd_a_log"].rearrange("o h -> h o")).then_inc(s_in, 16)
            sp.dma_start(crow[:], io["state_ssm_conv"][0].rearrange("b t c -> (b t) c")).then_inc(r_in, 16)
            sp.wait_ge(nc_d, 1)
            sp.dma_start(scr["negc"], negc[:]).then_inc(saved, 16)
            sp.wait_ge(pad_d, 1)
            sp.dma_start(scr["we"], we[:]).then_inc(saved, 16)
            sp.wait_ge(saved, 32)

        @block.scalar
        def _(act):
            st = Steps(act, act_s)
            act.wait_ge(s_in, 32)
            act.activation(par[:, 1:2], par[:, 1:2], ACT.Exp)
            act.wait_ge(u_d, 1)
            st.then_wait(act.activation(au[:], dt[:], ACT.Abs))
            st.then_wait(act.activation(au[:], au[:], ACT.Exp, scale=-1.0))
            act.activation(au[:], au[:], ACT.Ln, bias=1.0).then_inc(sp_d, 1)
            act.wait_ge(wx_d, 1)
            act.activation(wx[:], wx[:], ACT.Exp)
            act.activation(we[:, TS:2 * TS], we[:, TS:2 * TS], ACT.Exp).then_inc(wx_e, 1)

        @block.tensor
        def _(pe):
            pe.wait_ge(r_in, 16)
            for t in range(CT):
                i = pe.transpose(core.bank[5 + t // 16][:, 24 * (t % 16):24 * (t % 16) + 24], crow[:, t * P:(t + 1) * P],
                                 core.ident[0:24, 0:24])
            i.then_inc(turned, 1)
            pe.wait_ge(pad_d, 1)
            for n in range(K_N):
                i = pe.transpose(core.bank[1 + n // 8][:, 64 * (n % 8):64 * (n % 8) + 64], pad[:, n * P:(n + 1) * P],
                                 core.ident[0:64, 0:64])
            i.then_inc(turned, 1)

        @block.vector
        def _(dve):
            st = Steps(dve, dve_s)
            dve.memset(pad[:], 0.0)
            st.then_wait(dve.tensor_copy(keep2[:], core.keep[0:64]))
            dve.memset(keep2[:, P:P + 1], 0.0)
            dve.wait_ge(s_in, 32)
            dve.tensor_scalar(dt[:], core.bank[0][0:64, 0:T], par[:, 0:1], None, ALU.add).then_inc(u_d, 1)
            dve.wait_ge(sp_d, 1)
            st.then_wait(dve.scalar_tensor_tensor(dt[:], dt[:], 0.0, au[:], ALU.max, ALU.add))
            st.then_wait(dve.tensor_scalar(c[:], dt[:], par[:, 1:2], None, ALU.mult))
            st.then_wait(dve.tensor_tensor_scan(c[:], keep2[:], c[:], 0.0, ALU.mult, ALU.add))
            cs = samples(c[:, S0:T])
            dve.tensor_scalar(negc[:], c[:], -1.0, None, ALU.mult).then_inc(nc_d, 1)
            dve.tensor_scalar(we[:, TS:2 * TS], c[:, S0:T], -1.0, None, ALU.mult)
            st.then_wait(dve.tensor_tensor(tot[:], c[:, P - 1:P], c[:, TP - 1:TP], ALU.add))
            dve.tensor_scalar(wx[:, 0:P], c[:, 0:P], tot[:], None, ALU.subtract)
            dve.tensor_scalar(wx[:, P:TP], c[:, P:TP], c[:, TP - 1:TP], None, ALU.subtract)
            dve.tensor_tensor(samples(wx[:, S0:T]), cs, cs[:, :, TD - 1:TD].broadcast_to([64, NB, TD]), ALU.subtract
                              ).then_inc(wx_d, 1)
            dve.tensor_copy(pad[:, 0:TP], c[:, 0:TP])
            dve.tensor_copy(pad[:, K_CS * P + 96:K_CS * P + P], c[:, S0:T])
            dve.tensor_scalar(pad[:, K_C01 * P:K_C01 * P + P], c[:, 0:P], c[:, P - 1:P], None, ALU.subtract)
            dve.tensor_copy(pad[:, K_D0 * P:K_D0 * P + TP], dt[:, 0:TP])
            dve.tensor_copy(pad[:, K_DS * P + 96:K_DS * P + P], dt[:, S0:T])
            dve.wait_ge(wx_e, 1)
            dve.tensor_tensor(pad[:, K_W0 * P:K_W0 * P + TP], wx[:, 0:TP], dt[:, 0:TP], ALU.mult)
            dve.tensor_tensor(we[:, 0:TS], wx[:, S0:T], dt[:, S0:T], ALU.mult).then_inc(pad_d, 1)
            dve.wait_ge(turned, 1)
            for i in range(3):
                dve.tensor_copy(g["hist"][:, 16 * i:16 * i + 16].rearrange("p t c -> p (t c)"), core.bank[5 + i][:, 0:384])
            dve.wait_ge(turned, 2)
            dve.tensor_copy(g["cols"][:, 0:8].rearrange("p n h -> p (n h)"), core.bank[1][:, :])
            st.then_wait(dve.tensor_copy(g["cols"][:, 8], core.bank[2][:, 0:64]))


def ssd_mixer(nc, core, io, out, scr, g, ws):
    with ExitStack() as tmp:
        sb = lambda n, s, d=F32: core.sb("ssd_" + n, s, d, tmp)
        sem = lambda n: nc.alloc_semaphore(name="ssd_" + n)
        CP = 3 + TP + NB * 7
        CL = CP - 3
        xp, cy, cth = (sb(n, [P, 6, CP]) for n in ("conv_in", "conv_out", "conv_tanh"))
        xbc = sb("xbc", [P, 6, T])
        z = sb("z", [P, 4, T])
        nb = sb("neg_c", [P, 8, T])
        zt, sq = nb[:, 4:8], nb[:, 0:4]
        we = sb("we", [P, 4, 2 * TS])
        PP = sb("decay", [P, 8, 416])
        cbm = sb("cb_masked", [P, 416])
        xdt, xw = sb("x_dt_rows", [P, 2, 512]), sb("x_w_rows", [P, 2, 512])
        stack, bstack = sb("x_stack", [P, 4, P]), sb("b_stack", [P, 96])
        xw3, xsr = sb("xw3", [96, 512], F32R), sb("x_sample_rows", [P, 512])
        brow, b3m = sb("b_rows", [P, 2, P]), sb("b3m", [96, NB, P], F32R)
        stT, state = sb("state_turned", [P, 2, 512]), sb("state", [P, NB, 4, SSD_N])
        y = sb("y", [P, 4, T])
        inter = sb("inter", [P, 4, TS])
        var, r, t1 = (sb(n, [P, T]) for n in ("var", "r", "t1"))
        pst = sb("prompt_state", [P, 4, P])
        tail = sb("tail", [P, 6, 27])
        tailr = stT[:].rearrange("p s c -> p (s c)")[0:27, 0:768]
        cw, cc, wn, dd = sb("conv_w", [P, 6, 5]), sb("cols_cur", [P, K_N, 8]), sb("norm_w", [P, 4]), sb("d_cur", [P, 4])
        s = {n: sem(n) for n in ("proj_free conv_in_used conv tanh prep stacks nb_in args exps decays we_in we_used "
                                 "st_used brow xsd tanh_z zg gated squared o_ready o_stored r_first pst_out pst_stored "
                                 "tails tail_out upd dve act pool_w").split()}
        b_arrived = [sem(f"b_arrived{j}") for j in range(RAW)]
        full = [sem(f"bank{4 + i}_full") for i in range(4)]
        free = [sem(f"bank{4 + i}_free") for i in range(4)]
        st_in, st_out = [sem(f"state_in{i}") for i in range(2)], [sem(f"state_out{i}") for i in range(2)]
        block = tmp.enter_context(nc.Block())
        B = core.bank
        pairs = [(B[0], B[1]), (B[2], B[3])]
        wv = io["w_in_c"][0].rearrange("(k p) c -> p k c", p=P)
        NG, SL = SSD_G, 5
        RING = ["x0", "x1", "stack", "brow"] + [f"st{b}" for b in range(4)] + [f"u{i}" for i in range(4)]
        RING += [f"st{b}" for b in range(4, 8)] + [f"u{i}" for i in range(4, 8)] + [f"y{q}" for q in range(4)]
        OWN = ["cb", "inter", "pstate", "tail_x", "tail_bc", "rms"]

        def at(job, G):
            if job in RING:
                n = RING.index(job)
                return 1 + n % 3, G * (len(RING) // 3) + n // 3
            if isinstance(G, int) and G == -1:
                return 0, OWN.index(job) - 3
            n = OWN.index(job)
            if isinstance(G, int) and G == NG - 1 and n > 3:
                n -= 2
            return 0, G * len(OWN) + 2 + n

        def wait_free(eng, job, G):
            b, n = at(job, G)
            if not (isinstance(n, int) and n == 0):
                eng.wait_ge(free[b], n)

        def wait_read(eng, job, G):
            b, n = at(job, G)
            eng.wait_ge(free[b], n + 1)

        def wait_full(eng, job, G):
            b, n = at(job, G)
            eng.wait_ge(full[b], n + 1)
            return B[4 + b]

        def fill(job):
            return B[4 + at(job, 0)[0]], full[at(job, 0)[0]]

        TAIL_STEPS = (14, 16)

        def turns(eng):
            yield 0, None
            with eng.Fori(1, NG) as gg:
                yield gg, gg - 1
            yield None, NG - 1

        def load_group(sp, gg):
            for i in range(SL):
                if isinstance(gg, int) and gg == 0 and i == 0:
                    continue
                for j in range(UNITS):
                    k = slice(UK * j, UK * j + UK)
                    quad = gg * SL + (Q_SSD + i)
                    if i == 2:
                        srcs = [wv[:, k, bass.ds(gg * P + (8192 + 1024 * t), P)] for t in range(2)]
                        sp.wait_ge(ws["split"], quad * UNITS + (j + 1))
                        sp.sem_inc(ws["turns"], 1)
                        for t, arrived in ((0, b_arrived[j % RAW]), (1, ws["arrived"][j % RAW])):
                            sp.dma_start(core.w_raw[:, j % RAW, :, t * P:(t + 1) * P], srcs[t]).then_inc(arrived, 16)
                    else:
                        c0 = (4096, 4096 + GW, None, 0, GW)[i]
                        load_unit(sp, core, ws, quad, j, wv[:, k, bass.ds(gg * 512 + c0, GW)])

        @block.sync
        def _(sp):
            load_group(sp, 0)
            with sp.Fori(1, NG) as gg:
                load_group(sp, gg)
            wo = io["w_out_c"][0].rearrange("(k p) c -> p k c", p=P)
            for j in range(UNITS):
                load_unit(sp, core, ws, Q_OUT_C, j, wo[:, UK * j:UK * j + UK, 0:GW])

        def pool_wait(pool, sm, value):
            pool.wait_ge(sm, value)
            pool.sem_inc(s["pool_w"], 1)

        rows_of = lambda ap: ap.rearrange("b h p n -> b (h p) n")
        ssm_in, ssm_out = rows_of(io["state_ssm"][0]), rows_of(out["ssm_s"][0])

        def load_state(pool, gg, half):
            for b in range(4 * half, 4 * half + 4):
                pool.dma_start(state[:, b], ssm_in[b, bass.ds(gg * 512, 512), :].rearrange("(q p) n -> p q n", p=P)
                               ).then_inc(st_in[half], 16)

        def store_state(pool, gg, half):
            pool_wait(pool, s["upd"], gg * 8 + (4 * half + 4))
            for b in range(4 * half, 4 * half + 4):
                pool.dma_start(ssm_out[b, bass.ds(gg * 512, 512), :].rearrange("(q p) n -> p q n", p=P), state[:, b]
                               ).then_inc(st_out[half], 16)

        def load_nb(pool, gg):
            pool.dma_start(nb[:], scr["negc"][bass.ds(gg * 8, 8), :].partition_broadcast(P)).then_inc(s["nb_in"], 16)

        def load_we(pool, gg):
            v = scr["we"].rearrange("(a two) t -> two a t", two=2)
            for hh in range(2):
                pool.dma_start(we[64 * hh:64 * hh + 64], v[hh, bass.ds(gg * 4, 4), :].partition_broadcast(64)).then_inc(s["we_in"], 16)

        def store_tails(pool, gg):
            pool_wait(pool, free[0], at("tail_bc", gg - 1)[1] + 1)
            cs = out["scv_s"][0].rearrange("b t c -> (b t) c")
            for o, rows in ((out["scv_p"][0, 0], slice(0, 3)), (cs, slice(3, 27))):
                pool.dma_start(o[:, bass.ds(gg * 512, 512)], tailr[rows, 0:512]).then_inc(s["tail_out"], 16)
                for i in range(2):
                    pool.dma_start(o[:, bass.ds(gg * P + 4096 + 1024 * i, P)], tailr[rows, 512 + P * i:640 + P * i]
                                   ).then_inc(s["tail_out"], 16)

        def pool_scan(pool, G, nxt):
            for half in range(2):
                store_state(pool, G, half)
                if nxt is not None:
                    pool_wait(pool, st_out[half], nxt * 64)
                    load_state(pool, nxt, half)
            if nxt is not None:
                pool_wait(pool, s["we_used"], nxt)
                load_we(pool, nxt)
            pool_wait(pool, s["pst_out"], G + 1)
            pool.dma_start(rows_of(out["ssm_p"][0])[0, bass.ds(G * 512, 512), :].rearrange("(q p) n -> p q n", p=P), pst[:]
                           ).then_inc(s["pst_stored"], 16)
            if nxt is not None:
                store_tails(pool, nxt)
                pool_wait(pool, full[0], at("rms", G)[1] + 1)
                load_nb(pool, nxt)
            pool_wait(pool, s["o_ready"], G + 1)
            pool.dma_start(scr["oT"][:, bass.ds(G * 4, 4)], y[:]).then_inc(s["o_stored"], 16)

        @block.gpsimd
        def _(pool):
            load_nb(pool, 0)
            load_we(pool, 0)
            load_state(pool, 0, 0)
            load_state(pool, 0, 1)
            store_tails(pool, 0)
            with pool.Fori(0, NG - 1) as G:
                pool_scan(pool, G, G + 1)
            pool_scan(pool, NG - 1, None)
            pool_wait(pool, st_out[0], 64 * NG)
            pool_wait(pool, st_out[1], 64 * NG)
            pool_wait(pool, s["pst_stored"], 16 * NG)
            pool_wait(pool, s["o_stored"], 16 * NG)
            pool_wait(pool, s["tail_out"], 96 * NG)

        mm = lambda pe, *a, **k: pe.matmul(*a, skip_group_check=True, **k)

        def t_cb(pe, G):
            bk, full_ = fill("cb")
            wait_free(pe, "cb", G)
            bt, ct = xbc[:, 4], xbc[:, 5]
            mm(pe, bk[:, 0:256], bt[:, 0:P], ct[:, 0:TP], start=True, stop=True)
            mm(pe, bk[:, 256:384], bt[:, P:TP], ct[:, P:TP], start=True, stop=True)
            mm(pe, bk[96:128, 384:416], bt[:, S0:T], ct[:, S0:T], start=True, stop=True).then_inc(full_, 1)

        def t_x(pe, J, G):
            bk, full_ = fill(f"x{J}")
            if J == 0:
                pe.wait_ge(s["prep"], G + 1)
            wait_free(pe, f"x{J}", G)
            for q in range(4):
                i = pe.transpose(bk[:, q * P:(q + 1) * P], xbc[:, q, J * P:(J + 1) * P], core.ident[:])
            i.then_inc(full_, 1)

        def t_stack(pe, G):
            pe.wait_ge(s["stacks"], G + 1)
            bk, full_ = fill("stack")
            wait_free(pe, "stack", G)
            for q in range(4):
                i = pe.transpose(bk[:, q * P:(q + 1) * P], stack[:, q], core.ident[:])
            i.then_inc(full_, 1)

        def t_brow(pe, G):
            bk, full_ = fill("brow")
            wait_free(pe, "brow", G)
            for J in range(2):
                pe.transpose(bk[:, J * P:(J + 1) * P], xbc[:, 4, J * P:(J + 1) * P], core.ident[:])
            pe.transpose(bk[0:96, 256:384], bstack[:], core.ident[:]).then_inc(full_, 1)

        def t_state(pe, b, G):
            bk, full_ = fill(f"st{b}")
            wait_free(pe, f"st{b}", G)
            pe.wait_ge(st_in[b // 4], G * 64 + 64)
            for q in range(4):
                i = pe.transpose(bk[:, q * P:(q + 1) * P], state[:, b, q], core.ident[:])
            i.then_inc(full_, 1)

        def t_inter(pe, b, G):
            bk, full_ = fill("inter")
            if b == 0:
                wait_free(pe, "inter", G)
            wait_read(pe, f"st{b}", G)
            for q in range(4):
                i = mm(pe, bk[:, q * TS + TD * b:q * TS + TD * b + TD], stT[:, b % 2, q * P:(q + 1) * P],
                       xbc[:, 5, S0 + TD * b:S0 + TD * b + TD], start=True, stop=True)
            i.then_inc(s["st_used"] if b < NB - 1 else full_, 1)

        def t_update(pe, i, G):
            bk, full_ = fill(f"u{i}")
            wait_free(pe, f"u{i}", G)
            if i == 0:
                wait_read(pe, "brow", G)
            q, half = i % 4, i // 4
            pe.matmul(bk[:, :], xw3[:, q * P:(q + 1) * P], b3m[:, 4 * half:4 * half + 4].rearrange("p b n -> p (b n)"),
                      start=True, stop=True).then_inc(full_, 1)

        def t_pstate(pe, G):
            bk, full_ = fill("pstate")
            wait_free(pe, "pstate", G)
            wait_read(pe, "x1", G)
            wait_read(pe, "brow", G)
            for q in range(4):
                for J in range(2):
                    i = pe.matmul(bk[:, q * P:(q + 1) * P], xw[:, J, q * P:(q + 1) * P], brow[:, J], start=J == 0, stop=J == 1)
            i.then_inc(full_, 1)

        def t_y(pe, q, G):
            bk, full_ = fill(f"y{q}")
            wait_free(pe, f"y{q}", G)
            pe.wait_ge(s["decays"], G * 4 + (q + 1))
            if q == 0:
                pe.wait_ge(s["xsd"], G + 1)
            for hh in range(2):
                h = 2 * q + hh
                o, c = slice(64 * hh, 64 * hh + 64), slice(64 * h, 64 * h + 64)
                mm(pe, bk[o, 0:256], xdt[:, 0, c], PP[:, h, 0:256], start=True, stop=False)
                mm(pe, bk[o, 128:256], xdt[:, 1, c], PP[:, h, 256:384], start=False, stop=True)
                i = mm(pe, bk[o, S0:T], xsr[96:128, c], PP[96:128, h, 384:416], start=True, stop=True)
            i.then_inc(full_, 1)

        def t_tail(pe, part, gg):
            job = ("tail_x", "tail_bc")[part]
            bk, full_ = fill(job)
            wait_free(pe, job, gg - 1)
            pe.wait_ge(s["tails"], gg + 1)
            for i, t in enumerate((range(4), range(4, 6))[part]):
                ins = pe.transpose(bk[0:27, i * P:(i + 1) * P], tail[:, t], core.ident[:])
            ins.then_inc(full_, 1)

        def t_rms(pe, G):
            bk, full_ = fill("rms")
            wait_free(pe, "rms", G)
            pe.wait_ge(s["squared"], G * 4 + 4)
            for q in range(4):
                i = pe.matmul(bk[:, 0:T], core.ones[:], sq[:, q], start=q == 0, stop=q == 3)
            i.then_inc(full_, 1)

        T_STEPS = {0: ("x0", "x1"), 1: ("stack", "cb"), 2: ("brow", "st0"), 3: ("st1", "in0", "st2"),
                   4: ("in1", "st3", "in2"), 5: ("u0", "u1", "in3"), 6: ("u2", "u3"), 7: ("st4", "st5"), 8: ("st6", "in4", "in5"),
                   9: ("st7", "in6"), 10: ("u4", "u5", "in7"), 11: ("u6", "u7"), 12: ("y0",), 13: ("pstate", "y1"),
                   14: ("y2",), 15: ("y3",), 18: ("rms",)}

        def t_step(pe, k, G):
            for job in T_STEPS.get(k, ()):
                if job == "cb":
                    t_cb(pe, G)
                elif job in ("x0", "x1"):
                    t_x(pe, int(job[1]), G)
                elif job == "stack":
                    t_stack(pe, G)
                elif job == "brow":
                    t_brow(pe, G)
                elif job == "pstate":
                    t_pstate(pe, G)
                elif job == "rms":
                    t_rms(pe, G)
                elif job[:2] == "st":
                    t_state(pe, int(job[2:]), G)
                elif job[:2] == "in":
                    t_inter(pe, int(job[2:]), G)
                elif job[0] == "u":
                    t_update(pe, int(job[1:]), G)
                else:
                    t_y(pe, int(job[1:]), G)

        @block.tensor
        def _(pe):
            for gg, G in turns(pe):
                for i in range(SL):
                    if gg is not None:
                        n = gg * SL + (i - 1)
                        if i > 1 or (i == 1 and not isinstance(gg, int)):
                            pe.wait_ge(s["proj_free"], n)
                    for j in range(UNITS):
                        if G is not None and i == 0 and j == 0:
                            t_step(pe, 0, G)
                        if gg is not None and i == 0 and j == 0 and not isinstance(gg, int):
                            pe.wait_ge(s["proj_free"], gg * SL)
                        if gg is not None:
                            project_unit(pe, core, ws, gg * SL + (Q_SSD + i), j, core.xn_hi, core.xn_lo, 0, pairs[i % 2], True, True)
                            if 4 * i + j in TAIL_STEPS:
                                t_tail(pe, TAIL_STEPS.index(4 * i + j), gg)
                        if G is not None and i + j > 0:
                            t_step(pe, 4 * i + j, G)

        def a_evac(act, gg, i):
            act.wait_ge(ws["used"], gg * (SL * UNITS) + (Q_SSD + i + 2) * UNITS)
            if i == 0:
                act.wait_ge(s["conv_in_used"], gg + 1)
            if i == 3:
                act.wait_ge(s["zg"], gg)
            for m in range(2):
                bk = pairs[i % 2][m]
                if i < 3:
                    act.activation(xp[:, 2 * i + m, 3:3 + TP], bk[:, 0:TP], ACT.Copy)
                    ins = act.activation(samples(xp[:, 2 * i + m, 3 + TP:], 7)[:, :, 3:7], samples(bk[:, S0:T]), ACT.Copy)
                else:
                    ins = act.activation(z[:, 2 * i - 6 + m], bk[:, 0:T], ACT.Copy)
            ins.then_inc(s["proj_free"], 1)

        def a_step(act, k, G, st):
            if k == 1:
                bk = wait_full(act, "stack", G)
                act.activation(xw3[:], bk[0:96, :], ACT.Copy)
                act.activation(xsr[96:128], bk[96:128, :], ACT.Copy).then_inc(free[at("stack", 0)[0]], 1)
            if k == 2:
                bk = wait_full(act, "brow", G)
                act.activation(brow[:].rearrange("p j n -> p (j n)"), bk[:, 0:256], ACT.Copy).then_inc(s["brow"], 1)
            for b in {2: (0,), 3: (1, 2), 4: (3,), 7: (4, 5), 8: (6,), 9: (7,)}.get(k, ()):
                bk = wait_full(act, f"st{b}", G)
                if b >= 2:
                    act.wait_ge(s["st_used"], G * 7 + (b - 1))
                else:
                    act.wait_ge(s["tail_out"], (G + 1) * 96)
                act.activation(stT[:, b % 2], bk[:, :], ACT.Copy).then_inc(free[at(f"st{b}", 0)[0]], 1)
            if k in (5, 6):
                for q in ((0, 1), (2, 3))[k - 5]:
                    act.wait_ge(s["args"], G * 4 + (q + 1))
                    act.activation(PP[:, 2 * q:2 * q + 2], PP[:, 2 * q:2 * q + 2], ACT.Exp).then_inc(s["exps"], 1)
            if k == 7:
                act.wait_ge(s["args"], G * 4 + 4)
                act.wait_ge(s["proj_free"], G * SL + SL)
                act.activation(zt, z[:], ACT.Tanh, scale=0.5).then_inc(s["tanh_z"], 1)
            if k == 13:
                bk = wait_full(act, "pstate", G)
                act.wait_ge(s["pst_stored"], G * 16)
                act.activation(pst[:].rearrange("p q n -> p (q n)"), bk[:, :], ACT.Copy).then_inc(s["pst_out"], 1)
                act.wait_ge(s["pst_out"], G + 1)
                act.sem_inc(free[0], 1)
            if 13 <= k <= 16:
                q = k - 13
                act.wait_ge(s["gated"], G * 4 + (q + 1))
                act.activation(sq[:, q], y[:, q], ACT.Square, scale=0.5).then_inc(s["squared"], 1)
            if k == 19:
                act.wait_ge(free[0], at("rms", G)[1] + 1)
                rsqrt_act(act, r[:], var[:], st).then_inc(s["r_first"], 1)

        def a_prep(act, k, gg, st):
            if k in TAIL_STEPS:
                part = TAIL_STEPS.index(k)
                job = ("tail_x", "tail_bc")[part]
                bk = wait_full(act, job, gg - 1)
                if part == 0:
                    act.wait_ge(s["tail_out"], gg * 96)
                n0, n = ((0, 512), (512, 256))[part]
                act.activation(tailr[:, n0:n0 + n], bk[0:27, 0:n], ACT.Copy).then_inc(free[0], 1)
            if k == 16:
                act.wait_ge(s["conv"], gg + 1)
                act.activation(cth[:, :, 0:CL], cy[:, :, 0:CL], ACT.Tanh).then_inc(s["tanh"], 1)

        @block.scalar
        def _(act):
            st = Steps(act, s["act"])
            for gg, G in turns(act):
                st.restart()
                for i in range(SL):
                    for j in range(UNITS):
                        if G is not None and i == 0 and j == 0:
                            a_step(act, 0, G, st)
                        if gg is not None:
                            if i == 1:
                                act.wait_ge(b_arrived[j % RAW], gg * (16 * UNITS // RAW) + 16 * (j // RAW + 1))
                            split_hi_unit(act, core, ws, gg * SL + (Q_SSD + i + 1), j)
                            if j == UNITS - 1:
                                a_evac(act, gg, i)
                        if G is not None and i + j > 0:
                            a_step(act, 4 * i + j, G, st)
                        if gg is not None:
                            a_prep(act, 4 * i + j, gg, st)

        def v_prep(dve, k, gg, st):
            parts = ((slice(0, 4), gg * 4, 4), (slice(4, 5), gg + 32, 1), (slice(5, 6), gg + 40, 1))
            if k == 8:
                dve.wait_ge(s["conv_in_used"], gg + 1)
                for t, t0, n in parts:
                    hv = samples2(xp[:, t, 3 + TP:], 7)[:, :, :, 0:3]
                    dve.tensor_copy(hv, samples2(g["hist"][:, bass.ds(t0, n), :], 3))
                    for tap in range(5):
                        c0 = scw_col(tap) if tap < 4 else C_SCB
                        ins = dve.tensor_scalar(cw[:, t, tap], core.parT[:, bass.ds(t0 + c0, n)], 0.5, None, ALU.mult)
                st.then_wait(ins)
            if k == 12:
                dve.wait_ge(s["proj_free"], gg * SL + 3)
                dve.tensor_copy(tail[:, :, 0:3], xp[:, :, TP:TP + 3])
                dve.tensor_copy(tail[:, :, 3:27].rearrange("p m (b t) -> p m b t", t=3), samples2(xp[:, :, 3 + TP:], 7)[:, :, :, 4:7]
                                ).then_inc(s["tails"], 1)
            if 12 <= k <= 15:
                tap = k - 12
                for m in range(6):
                    w_ = cw[:, m, tap:tap + 1]
                    if tap == 0:
                        ins = dve.tensor_scalar(cy[:, m, 0:CL], xp[:, m, 0:CL], w_, cw[:, m, 4:5], ALU.mult, ALU.add)
                    else:
                        ins = dve.scalar_tensor_tensor(cy[:, m, 0:CL], xp[:, m, tap:tap + CL], w_, cy[:, m, 0:CL], ALU.mult, ALU.add)
                if tap < 3:
                    st.then_wait(ins)
                else:
                    ins.then_inc(s["conv"], 1)
                    dve.wait_ge(s["conv"], gg + 1)
                    dve.sem_inc(s["conv_in_used"], 1)
            if k == 17:
                dve.wait_ge(s["tanh"], gg + 1)
                dve.scalar_tensor_tensor(xbc[:, :, 0:TP], cth[:, :, 0:TP], 1.0, cy[:, :, 0:TP], ALU.add, ALU.mult)
                for m in range(6):
                    v7 = lambda x: samples(x[:, m, 3 + TP:], 7)[:, :, 0:TD]
                    ins = dve.scalar_tensor_tensor(samples(xbc[:, m, S0:T]), v7(cth), 1.0, v7(cy), ALU.add, ALU.mult)
                ins.then_inc(s["prep"], 1)
                dve.wait_ge(s["prep"], gg + 1)
                dve.wait_ge(s["we_in"], gg * 32 + 32)
                xs = xbc[:, 0:4, S0:T]
                dve.tensor_copy(stack[:, :, 96:128], xs)
                st.then_wait(dve.tensor_tensor(inter[:], xs, we[:, :, 0:TS], ALU.mult))
                hi = stack[:].bitcast(F32R)
                dve.tensor_copy(hi[:, :, 0:TS], inter[:])
                dve.tensor_copy(hi[:, :, TS:2 * TS], inter[:])
                b_ = xbc[:, 4, S0:T]
                bh = bstack[:].bitcast(F32R)
                dve.tensor_copy(bh[:, 0:TS], b_)
                st.then_wait(dve.tensor_copy(bh[:, 2 * TS:3 * TS], b_))
                dve.tensor_tensor(hi[:, :, 2 * TS:3 * TS], inter[:], stack[:, :, 0:TS], ALU.subtract)
                dve.tensor_tensor(bh[:, TS:2 * TS], b_, bstack[:, 0:TS], ALU.subtract).then_inc(s["stacks"], 1)
                dve.wait_ge(s["stacks"], gg + 1)

        def v_x(dve, J, G):
            bk = wait_full(dve, f"x{J}", G)
            v = bk[:].rearrange("p (h c) -> p h c", c=64)
            for dst, col in ((xdt, K_D0 + J), (xw, K_W0 + J)):
                ins = dve.tensor_tensor(dst[:, J].rearrange("p (h c) -> p h c", c=64), v,
                                        cc[:, col].unsqueeze(2).broadcast_to([P, 8, 64]), ALU.mult)
            ins.then_inc(free[at(f"x{J}", 0)[0]], 1)

        def v_args(dve, q):
            for h in (2 * q, 2 * q + 1):
                for c0, c1, i0, rows, col in ((0, 128, 0, slice(0, P), K_C0), (128, 256, 128, slice(0, P), K_C01),
                                              (256, 384, 128, slice(0, P), K_C1), (384, 416, S0, slice(96, P), K_CS)):
                    ins = dve.tensor_scalar(PP[rows, h, c0:c1], nb[rows, h, i0:i0 + c1 - c0], cc[rows, col, h:h + 1], 0.0,
                                            ALU.add, ALU.min)
            ins.then_inc(s["args"], 1)

        def v_decay(dve, q, G):
            dve.wait_ge(s["exps"], G * 4 + (q + 1))
            dve.tensor_tensor(PP[:, 2 * q:2 * q + 2], PP[:, 2 * q:2 * q + 2], cbm[:].unsqueeze(1).broadcast_to([P, 2, 416]),
                              ALU.mult).then_inc(s["decays"], 1)

        def v_update(dve, i, G, st):
            q, half = i % 4, i // 4
            bk = wait_full(dve, f"u{i}", G)
            for b in range(4):
                S = state[:, 4 * half + b, q]
                e = TS + TD * (4 * half + b) + TD - 1
                ins = dve.scalar_tensor_tensor(S, S, we[:, q, e:e + 1], bk[:, b * P:(b + 1) * P], ALU.mult, ALU.add)
            ins.then_inc(s["upd"], 1)
            dve.wait_ge(s["upd"], G * 8 + (i + 1))
            dve.sem_inc(free[at(f"u{i}", 0)[0]], 1)

        def v_y(dve, q, G, st):
            bk = wait_full(dve, f"y{q}", G)
            if q == 0:
                dve.wait_ge(s["o_stored"], G * 16)
            dve.scalar_tensor_tensor(y[:, q], xbc[:, q], dd[:, q:q + 1], bk[:, 0:T], ALU.mult, ALU.add
                                     ).then_inc(free[at(f"y{q}", 0)[0]], 1)
            wait_read(dve, f"y{q}", G)
            st.then_wait(dve.tensor_tensor(y[:, q, S0:T], y[:, q, S0:T], inter[:, q], ALU.add))
            dve.tensor_tensor(y[:, q], y[:, q], zt[:, q], ALU.mult).then_inc(s["gated"], 1)

        def v_step(dve, k, G, st):
            if k == 0:
                dve.wait_ge(s["gated"], G * 4)
                dve.tensor_copy(cc[:], g["cols"][:, :, bass.ds(G * 8, 8)])
                dve.tensor_scalar(wn[:], core.parT[:, bass.ds(G * 4 + C_SN, 4)], 0.5, None, ALU.mult)
                st.then_wait(dve.tensor_copy(dd[:], core.parT[:, bass.ds(G * 4 + C_D, 4)]))
                v_x(dve, 0, G)
                v_x(dve, 1, G)
            if k == 1:
                bk = wait_full(dve, "cb", G)
                dve.tensor_tensor(cbm[:, 0:128], bk[:, 0:128], core.tri[:], ALU.mult)
                dve.tensor_copy(cbm[:, 128:256], bk[:, 128:256])
                dve.tensor_tensor(cbm[:, 256:384], bk[:, 256:384], core.tri[:], ALU.mult)
                dve.tensor_tensor(cbm[96:128, 384:416], bk[96:128, 384:416], core.smask[96:128], ALU.mult).then_inc(free[0], 1)
                wait_read(dve, "cb", G)
                wait_read(dve, "stack", G)
                dve.tensor_tensor(xsr[96:128].rearrange("p (h c) -> p h c", c=64), xsr[96:128].rearrange("p (h c) -> p h c", c=64),
                                  cc[96:128, K_DS].unsqueeze(2).broadcast_to([32, 8, 64]), ALU.mult).then_inc(s["xsd"], 1)
            if k == 2:
                dve.wait_ge(s["brow"], G + 1)
                bk = wait_full(dve, "brow", G)
                dve.tensor_tensor(b3m[:], bk[0:96, 256:384].unsqueeze(1).broadcast_to([96, NB, P]),
                                  core.seg[0:96].unsqueeze(2).broadcast_to([96, NB, P]), ALU.mult).then_inc(free[at("brow", 0)[0]], 1)
            if k in (2, 3):
                if k == 2:
                    dve.wait_ge(s["nb_in"], G * 16 + 16)
                v_args(dve, 2 * k - 4)
                v_args(dve, 2 * k - 3)
            for i in {5: (0, 1), 6: (2, 3), 10: (4, 5), 11: (6, 7)}.get(k, ()):
                v_update(dve, i, G, st)
            for q in {7: (0, 1), 8: (2,), 9: (3,)}.get(k, ()):
                v_decay(dve, q, G)
            if k == 9:
                dve.wait_ge(s["tanh_z"], G + 1)
                st.then_wait(dve.scalar_tensor_tensor(zt, zt, 1.0, z[:], ALU.add, ALU.mult))
                dve.sem_inc(s["zg"], 1)
            if k == 11:
                bk = wait_full(dve, "inter", G)
                dve.tensor_tensor(inter[:], bk[:, 0:4 * TS].rearrange("p (q t) -> p q t", q=4),
                                  we[:, :, TS:2 * TS], ALU.mult).then_inc(free[0], 1)
                wait_read(dve, "inter", G)
                dve.sem_inc(s["we_used"], 1)
            if 12 <= k <= 15:
                v_y(dve, k - 12, G, st)
            if k == 16:
                dve.wait_ge(s["gated"], G * 4 + 4)
            if k == 18:
                bk = wait_full(dve, "rms", G)
                dve.tensor_scalar(var[:], bk[:, 0:T], 1.0 / 512, EPS, ALU.mult, ALU.add).then_inc(free[0], 1)
            if k == 19:
                dve.wait_ge(s["r_first"], G + 1)
                st.then_wait(rsqrt_newton(dve, r[:], var[:], t1[:], st))
                for q in range(4):
                    ins = dve.scalar_tensor_tensor(y[:, q], y[:, q], wn[:, q:q + 1], r[:], ALU.mult, ALU.mult)
                ins.then_inc(s["o_ready"], 1)
                dve.wait_ge(s["o_ready"], G + 1)

        @block.vector
        def _(dve):
            st = Steps(dve, s["dve"])
            dve.memset(cbm[0:96, 384:416], 0.0)
            dve.memset(PP[0:96, :, 384:416], 0.0)
            st.then_wait(dve.memset(xp[:, :, 0:3], 0.0))
            dve.sem_inc(s["conv_in_used"], 1)
            for gg, G in turns(dve):
                st.restart()
                for i in range(SL):
                    for j in range(UNITS):
                        if G is not None and i == 0 and j == 0:
                            v_step(dve, 0, G, st)
                        if gg is not None:
                            split_lo_unit(dve, core, ws, gg * SL + (Q_SSD + i + 1), j)
                        if G is not None and i + j > 0:
                            v_step(dve, 4 * i + j, G, st)
                        if gg is not None:
                            v_prep(dve, 4 * i + j, gg, st)


def program(nc, io, out):
    with ExitStack() as ctx:
        ctx.enter_context(nc.allow_non_contiguous_dma(reason="a few columns of gates"))
        core = Core(nc, ctx)
        scr = {n: nc.dram_tensor(f"scr_{n}", s, F32).ap() for n, s in
               (("x0T", [P, KT, T]), ("x1T", [P, KT, T]), ("oT", [P, 32, T]), ("gcum", [P, 8, T]), ("ml_rows", [4, R_N]),
                ("negc", [SSD_H, T]), ("we", [SSD_H, 2 * TS]))}
        ws = weight_sems(lambda n: ctx.enter_context(nc.semaphore(n)), "all")
        with ExitStack() as layer:
            g = layer0_buffers(core, layer)
            with ExitStack() as early:
                gw = gate_weights(core, early)
                with nc.cleanup_on_exit():
                    setup(nc, core, io, scr, gw)
                with nc.cleanup_on_exit():
                    gates0(nc, core, io, out, scr, g, ws)
            with nc.cleanup_on_exit():
                ab_mixers(nc, core, io, out, scr, g, ws)
        with ExitStack() as layer:
            g = layer1_buffers(core, layer)
            with ExitStack() as early:
                gw = core.sb("dt_w", [P, KT, 64], F32, early)
                with nc.cleanup_on_exit():
                    out_proj(nc, core, io, out, scr, ws, last=False, gw=gw)
                with nc.cleanup_on_exit():
                    gates1(nc, core, io, scr, g)
            with nc.cleanup_on_exit():
                ssd_mixer(nc, core, io, out, scr, g, ws)
        with nc.cleanup_on_exit():
            out_proj(nc, core, io, out, scr, ws, last=True)


_INS = ["x_prompt", "x_sample", "state_gla", "state_mlstm_c", "state_mlstm_n", "state_mlstm_m", "state_mlstm_conv",
        "state_ssm", "state_ssm_conv", "norm_ab", "w_in_ab", "gla_w_a2", "gla_b_a", "gla_norm", "mlstm_conv_w",
        "mlstm_conv_b", "mlstm_b_i", "mlstm_b_f", "mlstm_norm", "w_out_ab", "norm_c", "w_in_c", "ssd_conv_w",
        "ssd_conv_b", "ssd_dt_bias", "ssd_a_log", "ssd_d", "ssd_norm", "w_out_c", "final_norm"]
_OUTS = [("y_p", (1, TP, D)), ("y_s", (NB, TD, D)), ("gla_p", (1, 1, 4, DK, DV)), ("gla_s", (1, NB, 4, DK, DV)),
         ("mc_p", (1, 1, 4, DK, DV)), ("mc_s", (1, NB, 4, DK, DV)), ("mn_p", (1, 1, 4, DK)), ("mn_s", (1, NB, 4, DK)),
         ("mm_p", (1, 1, 4)), ("mm_s", (1, NB, 4)), ("mcv_p", (1, 1, 3, 2048)), ("mcv_s", (1, NB, 3, 2048)),
         ("ssm_p", (1, 1, SSD_H, SSD_P, SSD_N)), ("ssm_s", (1, NB, SSD_H, SSD_P, SSD_N)),
         ("scv_p", (1, 1, 3, 6144)), ("scv_s", (1, NB, 3, 6144))]


def kernel(**inputs):
    import concourse.bacc as bacc
    from concourse.bass_utils import run_bass_kernel_spmd

    nc = bacc.Bacc("TRN2", target_bir_lowering=False, num_devices=1)
    arrays, io = {}, {}
    for name in _INS:
        a = np.ascontiguousarray(inputs[name])
        arrays[f"in_{name}"] = a
        io[name] = nc.dram_tensor(f"in_{name}", a.shape, mybir.dt.from_np(a.dtype), kind="ExternalInput").ap()
    out = {n: nc.dram_tensor(f"out_{n}", shape, F32, kind="ExternalOutput").ap() for n, shape in _OUTS}
    program(nc, io, out)
    got = run_bass_kernel_spmd(nc, [arrays], core_ids=[0]).results[0]
    return tuple(got[f"out_{n}"] for n, _ in _OUTS)
```
